# Optimizing a Trainium2 kernel written in Bass

```python
import jax, jax.numpy as jnp
from jax import lax
import numpy as np

D_MODEL = 1024
BATCH = 1
SEQ = 1024
DEPTH = 2

N_HEADS_A = 8
HEAD_DIM = 64
WIDTH_A = N_HEADS_A * HEAD_DIM
N_IDX_HEADS = 8
IDX_DIM = 32
TOPK_MAX = 256
Q_BLOCK = 128
IDX_SCALE = (N_IDX_HEADS ** -0.5) * (IDX_DIM ** -0.5)
N_GROUPS_B = 8
GROUP_DIM_B = 64
WIDTH_B = N_GROUPS_B * GROUP_DIM_B
CHUNK = 128
IN_SPLITS = (WIDTH_A, HEAD_DIM, HEAD_DIM, N_IDX_HEADS * IDX_DIM, IDX_DIM, N_IDX_HEADS, WIDTH_B, WIDTH_B)
IN_WIDTH = WIDTH_A + 2 * HEAD_DIM + N_IDX_HEADS * IDX_DIM + IDX_DIM + N_IDX_HEADS + 2 * WIDTH_B
CONV_WIDTH = 31
D_FF = 4 * D_MODEL
ROPE_THETA = 10000.0
EPS = 1e-6
N_EVEN = (DEPTH + 1) // 2
N_ODD = DEPTH // 2

kernel_name = "hybrid_dsa_gmlp_conformer_block"

def rms_norm(x, g):
    xf = x.astype(jnp.float32)
    y = xf * lax.rsqrt(jnp.mean(xf * xf, axis=-1, keepdims=True) + EPS)
    return (y * g.astype(jnp.float32)).astype(x.dtype)

def rope(x, positions):
    d = x.shape[-1]
    half = d // 2
    inv_freq = ROPE_THETA ** (-jnp.arange(half, dtype=jnp.float32) * 2.0 / d)
    ang = positions.astype(jnp.float32)[..., None] * inv_freq
    cos = jnp.cos(ang)[:, :, None, :]
    sin = jnp.sin(ang)[:, :, None, :]
    xf = x.astype(jnp.float32)
    x1, x2 = xf[..., :half], xf[..., half:]
    out = jnp.concatenate([x1 * cos - x2 * sin, x2 * cos + x1 * sin], axis=-1)
    return out.astype(x.dtype)

def split_columns(z, sizes):
    outs, start = [], 0
    for s in sizes:
        outs.append(z[..., start:start + s])
        start += s
    return outs

def dsa_attention(q, k, v, qi, ki, wi):
    B, S = q.shape[0], q.shape[1]
    topk = min(TOPK_MAX, S // 4)
    nb = S // Q_BLOCK
    key_pos = jnp.arange(S)
    ki32 = ki.astype(jnp.float32)

    def to_blocks(a):
        return a.reshape((B, nb, Q_BLOCK) + a.shape[2:]).swapaxes(0, 1)

    def block_fn(args):
        blk, qb, qib, wib = args
        t = blk * Q_BLOCK + jnp.arange(Q_BLOCK)
        causal = key_pos[None, :] <= t[:, None]
        logits = jnp.einsum('bqhe,bse->bqhs', qib.astype(jnp.float32), ki32)
        score = jnp.einsum('bqh,bqhs->bqs', wib.astype(jnp.float32), jax.nn.relu(logits))
        score = jnp.where(causal[None], score, -jnp.inf)
        _, idx = lax.top_k(score, topk)
        k_sel = jax.vmap(lambda kk, ii: kk[ii])(k, idx)
        v_sel = jax.vmap(lambda vv, ii: vv[ii])(v, idx)
        valid = idx <= t[None, :, None]
        att = jnp.einsum('bqhd,bqkd->bqhk', qb.astype(jnp.float32),
                         k_sel.astype(jnp.float32)) * (HEAD_DIM ** -0.5)
        att = jnp.where(valid[:, :, None, :], att, -jnp.inf)
        p = jax.nn.softmax(att, axis=-1)
        out = jnp.einsum('bqhk,bqkd->bqhd', p, v_sel.astype(jnp.float32))
        return out.astype(qb.dtype)

    out = lax.map(block_fn, (jnp.arange(nb), to_blocks(q), to_blocks(qi), to_blocks(wi)))
    return out.swapaxes(0, 1).reshape(B, S, -1)

def spatial_gating(uv, g_v, w_s, b_s):
    B, S = uv.shape[0], uv.shape[1]
    u, vv = uv[..., :WIDTH_B], uv[..., WIDTH_B:]
    vv = rms_norm(vv, g_v)
    vv = vv.reshape(B, S // CHUNK, CHUNK, N_GROUPS_B, GROUP_DIM_B)
    w = w_s * jnp.tril(jnp.ones((CHUNK, CHUNK), dtype=w_s.dtype))[None]
    sv = jnp.einsum('gij,bcjgd->bcigd', w, vv) + b_s.T[None, None, :, :, None]
    return u * sv.reshape(B, S, WIDTH_B)

def even_layer(x, positions, g_norm, w_in, g_q, g_k, g_kidx, g_vb, w_s, b_s, w_out):
    B, S, _ = x.shape
    h = rms_norm(x, g_norm)
    z = h @ w_in
    q, k, v, qi, ki, wi, u, vb = split_columns(z, IN_SPLITS)
    q = rope(rms_norm(q.reshape(B, S, N_HEADS_A, HEAD_DIM), g_q), positions)
    k = rope(rms_norm(k, g_k)[:, :, None, :], positions)[:, :, 0]
    qi = rope(qi.reshape(B, S, N_IDX_HEADS, IDX_DIM), positions)
    ki = rope(rms_norm(ki, g_kidx)[:, :, None, :], positions)[:, :, 0]
    wi = wi * IDX_SCALE
    a_out = dsa_attention(q, k, v, qi, ki, wi)
    b_out = spatial_gating(jax.nn.gelu(jnp.concatenate([u, vb], axis=-1)), g_vb, w_s, b_s)
    return x + jnp.concatenate([a_out, b_out], axis=-1) @ w_out

def odd_layer(x, g_norm, w_pw1, w_dw, b_dw, g_conv, w_pw2):
    h = rms_norm(x, g_norm)
    z = h @ w_pw1
    y = z[..., :D_MODEL] * jax.nn.sigmoid(z[..., D_MODEL:])
    y = lax.conv_general_dilated(
        y, w_dw[:, None, :].astype(y.dtype), window_strides=(1,),
        padding=[(CONV_WIDTH - 1, 0)], dimension_numbers=('NWC', 'WIO', 'NWC'),
        feature_group_count=D_MODEL) + b_dw
    y = jax.nn.silu(rms_norm(y, g_conv))
    return x + y @ w_pw2

def channel_mixer(x, g_norm, w1, w2):
    h = rms_norm(x, g_norm)
    return x + jnp.square(jax.nn.relu(h @ w1)) @ w2

def setup_inputs(seed: int = 0) -> dict:
    key = jax.random.key(seed)
    ks = jax.random.split(key, 24)
    f32 = jnp.float32
    nrm = lambda k, shape, scale: jax.random.normal(k, shape, f32) * scale
    gain = lambda k, shape: 1.0 + 0.05 * jax.random.normal(k, shape, f32)
    x = jax.random.normal(ks[0], (BATCH, SEQ, D_MODEL), f32)
    offs = jax.random.randint(ks[1], (BATCH, 1), 0, 1024, dtype=jnp.int32)
    positions = (offs + jnp.arange(SEQ, dtype=jnp.int32)[None, :]).astype(jnp.int32)
    return {
        "x": x,
        "positions": positions,
        "ev_g_norm": gain(ks[2], (N_EVEN, D_MODEL)),
        "ev_w_in": nrm(ks[3], (N_EVEN, D_MODEL, IN_WIDTH), D_MODEL ** -0.5),
        "ev_g_q": gain(ks[4], (N_EVEN, HEAD_DIM)),
        "ev_g_k": gain(ks[5], (N_EVEN, HEAD_DIM)),
        "ev_g_kidx": gain(ks[6], (N_EVEN, IDX_DIM)),
        "ev_g_vb": gain(ks[7], (N_EVEN, WIDTH_B)),
        "ev_w_s": nrm(ks[8], (N_EVEN, N_GROUPS_B, CHUNK, CHUNK), 0.5 * CHUNK ** -0.5),
        "ev_b_s": 1.0 + nrm(ks[9], (N_EVEN, N_GROUPS_B, CHUNK), 0.05),
        "ev_w_out": nrm(ks[10], (N_EVEN, WIDTH_A + WIDTH_B, D_MODEL), (WIDTH_A + WIDTH_B) ** -0.5),
        "od_g_norm": gain(ks[11], (N_ODD, D_MODEL)),
        "od_w_pw1": nrm(ks[12], (N_ODD, D_MODEL, 2 * D_MODEL), D_MODEL ** -0.5),
        "od_w_dw": nrm(ks[13], (N_ODD, CONV_WIDTH, D_MODEL), CONV_WIDTH ** -0.5),
        "od_b_dw": nrm(ks[14], (N_ODD, D_MODEL), 0.01),
        "od_g_conv": gain(ks[15], (N_ODD, D_MODEL)),
        "od_w_pw2": nrm(ks[16], (N_ODD, D_MODEL, D_MODEL), D_MODEL ** -0.5),
        "ff_g_norm": gain(ks[17], (DEPTH, D_MODEL)),
        "ff_w1": nrm(ks[18], (DEPTH, D_MODEL, D_FF), D_MODEL ** -0.5),
        "ff_w2": nrm(ks[19], (DEPTH, D_FF, D_MODEL), 0.5 * D_FF ** -0.5),
    }

def reference(x, positions, ev_g_norm, ev_w_in, ev_g_q, ev_g_k, ev_g_kidx, ev_g_vb,
              ev_w_s, ev_b_s, ev_w_out, od_g_norm, od_w_pw1, od_w_dw, od_b_dw,
              od_g_conv, od_w_pw2, ff_g_norm, ff_w1, ff_w2):
    for layer in range(DEPTH):
        i = layer // 2
        if layer % 2 == 0:
            x = even_layer(x, positions, ev_g_norm[i], ev_w_in[i], ev_g_q[i], ev_g_k[i],
                           ev_g_kidx[i], ev_g_vb[i], ev_w_s[i], ev_b_s[i], ev_w_out[i])
        else:
            x = odd_layer(x, od_g_norm[i], od_w_pw1[i], od_w_dw[i], od_b_dw[i],
                          od_g_conv[i], od_w_pw2[i])
        x = channel_mixer(x, ff_g_norm[layer], ff_w1[layer], ff_w2[layer])
    return x


_drawn_inputs = setup_inputs


def setup_inputs(seed=0):
    import zlib

    import numpy as np

    out = dict(_drawn_inputs(seed))
    spreads = {}
    factors = {'ev_g_q': 8.0,
     'ev_g_k': 8.0,
     'ev_g_kidx': 5.064,
     'ev_g_vb': 7.143,
     'od_b_dw': 6.855,
     'ev_b_s': 4.107,
     'od_g_norm': 3.249,
     'od_g_conv': 3.043}
    for name, (base, spread) in spreads.items():
        noise = np.random.default_rng([zlib.crc32(name.encode()), seed]).standard_normal(out[name].shape)
        drawn = base * np.exp(spread * noise) if base else spread * noise
        out[name] = __import__('jax').numpy.asarray(drawn.astype(out[name].dtype))
    for name, factor in factors.items():
        out[name] = (out[name] * factor).astype(out[name].dtype)
    return out
```

```python
from contextlib import ExitStack

import numpy as np

import concourse.bass as bass
from concourse import mybir

ALU = mybir.AluOpType
ACT = mybir.ActivationFunctionType
F32 = mybir.dt.float32
F32R = mybir.dt.float32r
I32 = mybir.dt.int32
AX_X = mybir.AxisListType.X

P = 128
SEQ = 1024
D = 1024
KT = D // P
HALF = 512
HT = HALF // P
HEADS, HD = 8, 64
IH, ID = 8, 32
TOPK = 256
ROUNDS = TOPK // 8
GROUPS, GD = 8, 64
IDX_SCALE = (IH ** -0.5) * (ID ** -0.5)
CONV = 31
EPS = 1e-6
K0, V0, QI0, KI0, WI0 = 0, 64, 128, 384, 416
C0 = 424
CHUNK_COLS = [C0, 512, 512, 512]
KV, QC, UC, VC = range(4)
NSTEP = 32
NEG = -1e30
TAKEN = -3e38
G_EV, G_FF0, G_OD, G_CONV, G_FF1, B_DW = range(6)

ZB = 16
WOUT, FF0, PW1, PW2, FF1 = ZB, ZB + 8, ZB + 72, ZB + 88, ZB + 96
NBLOCK = ZB + 160
STAGES = [("wout", 0, WOUT, 8), ("ff0", 0, FF0, 64), ("pw1", 0, PW1, 16),
          ("wout", 1, WOUT, 8), ("ff0", 1, FF0, 64), ("pw1", 1, PW1, 16),
          ("pw2", 0, PW2, 8), ("ff1", 0, FF1, 64), ("pw2", 1, PW2, 8), ("ff1", 1, FF1, 64)]
FIRST = {}
_n = 0
for _name, _half, _block, _count in STAGES:
    FIRST[_name, _half] = _n
    _n += _count
NUNIT = _n
AHEAD = 3


def transposition_groups():
    groups = []
    for t in range(8):
        groups.append(("k", t, 0))
        if t >= 2:
            groups += [("qi", t, 0), ("qi", t, 1)]
    for t in range(8):
        groups += [("q", t, 0), ("q", t, 1)]
        if t % 4:
            groups += [("cat", t - 1, 0), ("cat", t - 1, 1)]
        for h in range(HEADS):
            groups += [("p", t, h, g) for g in range((t + 4) // 4)]
        if t % 4 == 3:
            groups += [("cat", t, 0), ("cat", t, 1)]
    return {key: n for n, key in enumerate(groups)}


TR = transposition_groups()
CATS = [n for key, n in TR.items() if key[0] == "cat"]
LOGITS = [0, 0, 0]
for _t in range(2, 8):
    LOGITS.append(LOGITS[-1] + IH * ((_t + 4) // 4))
UPS = {("ff0", 0): 0, ("ff0", 1): 32, ("ff1", 0): 64, ("ff1", 1): 96}
CONV_IN = {("ff0", 1): "conv0", ("ff1", 0): "conv1"}
CONSTS = 4
CREDIT = 2


def wait_apart(engine, sem, value, passed):
    engine.wait_ge(sem, value)
    engine.sem_inc(passed, 1)


def flat(buf, part, k):
    return buf[:, k, :] if part is None else buf[:, part, k, :]


def build(nc, x_t, positions, inv_freq, weights, gains, g_head, g_vb, w_s, b_s, w_dw, out_t):
    with ExitStack() as ctx:
        base = (nc.sbuf_base + 31) // 32 * 32

        def put(name, at, shape, dt=F32):
            size = int(np.prod(shape[1:])) * 4
            return nc.alloc_sbuf_tensor_at(name, shape, dt, offset=base + at), at + size

        KB = 1024
        h_buf, _ = put("h_buf", 0, [P, 2, KT, HALF], F32R)
        hid_buf, _ = put("hid_buf", 32 * KB, [P, 2, KT, HALF], F32R)
        w_buf, _ = put("w_buf", 64 * KB, [P, 2, KT, HALF], F32R)
        raw, _ = put("raw", 96 * KB, [P, 2, KT, P])
        xt0, _ = put("xt0", 104 * KB, [P, KT, HALF])
        xt1, _ = put("xt1", 120 * KB, [P, KT, HALF])
        xt = [xt0, xt1]
        x_in, a = put("x_in", 104 * KB, [P, 2, HALF])
        zt, a = put("zt", a, [P, C0])
        qz, a = put("qz", a, [P, HALF])
        tmp, a = put("tmp", a, [P, 2, HALF])
        k_stack, a = put("k_stack", a, [P, 3, HD], F32R)
        ki_stack, a = put("ki_stack", a, [P, 3, ID], F32R)
        qi_stack, a = put("qi_stack", a, [P, IH, 3, ID], F32R)
        assert a <= 120 * KB
        q_tok, _ = put("q_tok", 120 * KB, [P, 8, HEADS, HD])
        s_buf, a = put("s_buf", 0, [P, 2, SEQ])
        p_buf, a = put("p_buf", a, [P, 2, SEQ])
        pt_buf, a = put("pt_buf", a, [P, 2, SEQ])
        q_t, a = put("q_t", a, [P, HEADS, P], F32R)
        q_stack, a = put("q_stack", a, [P, HEADS, 2, HD], F32R)
        assert a <= 32 * KB
        k_t, a = put("k_t", 136 * KB, [P, SEQ], F32R)
        k_lo_t, a = put("k_lo_t", a, [HD, SEQ], F32R)
        v_tok, a = put("v_tok", a, [P, 8, HD])
        score = [None, None]
        for t in range(2, 8):
            s, a = put(f"score{t}", a, [P, P * (t + 1)])
            score.append(s)
        b_tok, a = put("b_tok", a, [P, 8, HALF])
        y_buf, c = put("y_buf", 136 * KB, [P, KT, CONV - 1 + HALF])
        c_buf, c = put("c_buf", c, [P, KT, HALF])
        assert c <= a
        ident, a = put("ident", a, [P, P])
        ones, a = put("ones", a, [P, P])
        tri, a = put("tri", a, [P, P])
        gain, a = put("gain", a, [P, 6, KT])
        wdw, a = put("wdw", a, [P, KT, CONV])
        small, a = put("small", a, [P, 112])
        sq_sum, a = put("sq_sum", a, [P, HALF])
        sq_ring, a = put("sq_ring", a, [P, 2, HALF])
        again = a
        qi_t, a = put("qi_t", again, [P, IH, P], F32R)
        ki_t, a = put("ki_t", a, [P, SEQ], F32R)
        ws, a = put("ws", a, [P, GROUPS, P])
        cos, a = put("cos", a, [P, 8, HD // 2])
        sin, a = put("sin", a, [P, 8, HD // 2])
        gvb, a = put("gvb", a, [P, HALF])
        gh, a = put("gh", a, [P, 3, HD])
        bs, a = put("bs", a, [P, GROUPS])
        pos_i, a = put("pos_i", a, [P, 8], I32)
        inv_f, a = put("inv_f", a, [P, HD // 2])
        end_z = a
        rms_bc, a = put("rms_bc", again, [P, HALF])
        conv_bc, a = put("conv_bc", a, [P, HALF])
        t_ring, a = put("t_ring", a, [P, 2, HALF])
        s_ring, a = put("s_ring", a, [P, 2, HALF])
        a_tok, a = put("a_tok", a, [P, HALF])
        c_sum, a = put("c_sum", a, [P, HALF])
        diag_buf, a = put("diag_buf", a, [P, HALF])
        assert max(a, end_z) + base <= nc.sbuf_usable_end, (a, end_z)

        diag = diag_buf[:]

        def yflat(k, at):
            return y_buf[:, k, at:at + HALF]

        def gflat(g, k):
            return gain[:, g, bass.ds(k, 1)]

        psum = nc.alloc_psum_tensor("psum", [P, 8, HALF], F32)

        pos_f = small[:, 0:8]
        r_tok = small[:, 8:16]
        st_v, st_y, st_a = small[:, 16:24], small[:, 24:32], small[:, 32:40]
        top8 = small[:, 48:56]
        row_sum = small[:, 56:64]
        neg_max = small[:, 64:66]
        row_max = small[:, 66:68]
        r_inv = small[:, 72:80]
        vsum = small[:, 80:81]
        w_idx = [small[:, 84 + 8 * n:92 + 8 * n] for n in range(3)]

        def sem(name):
            return ctx.enter_context(nc.semaphore(name))

        consts_in = sem("consts_in")
        consts_up = sem("consts_up")
        rope_up = sem("rope_up")
        rope_arg = sem("rope_arg")
        x_in_full = [sem("x_in_full0"), sem("x_in_full1")]
        landed = [sem("landed0"), sem("landed1")]
        hi_up = sem("hi_up")
        lo_up = sem("lo_up")
        prep_hi = sem("prep_hi")
        prep_sq = sem("prep_sq")
        prep_lo = sem("prep_lo")
        prep_sum = sem("prep_sum")
        sum_clear = sem("sum_clear")
        stat_up = sem("stat_up")
        stat_diag = sem("stat_diag")
        stat_bc = sem("stat_bc")
        z_up = sem("z_up")
        z_read = sem("z_read")
        z_proc = sem("z_proc")
        z_vsq = sem("z_vsq")
        tr_up = sem("tr_up")
        tr_read = sem("tr_read")
        logit_up = sem("logit_up")
        logit_relu = sem("logit_relu")
        logit_used = sem("logit_used")
        spat_up = sem("spat_up")
        spat_used = sem("spat_used")
        q_split = sem("q_split")
        qk_up = sem("qk_up")
        qk_masked = sem("qk_masked")
        neg_up = sem("neg_up")
        exp_up = sem("exp_up")
        pv_up = sem("pv_up")
        att_norm = sem("att_norm")
        cat_hi = sem("cat_hi")
        cat_lo = sem("cat_lo")
        unit_up = sem("unit_up")
        unit_read = sem("unit_read")
        squared = sem("squared")
        hid_hi = sem("hid_hi")
        hid_lo = sem("hid_lo")
        gate_up = sem("gate_up")
        y_up = sem("y_up")
        topk_step = sem("topk_step")
        conv_step = sem("conv_step")
        conv_sq = sem("conv_sq")
        conv_sum = sem("conv_sum")
        act_in = sem("act_in")
        act_silu = sem("act_silu")
        act_hi = sem("act_hi")
        act_lo = sem("act_lo")
        x_full = sem("x_full")
        out_sem = sem("out_sem")
        passed_v = sem("passed_v")
        passed_s = sem("passed_s")
        dve_chain = sem("dve_chain")
        act_chain = sem("act_chain")
        pool_chain = sem("pool_chain")

        block = ctx.enter_context(nc.Block())

        PREPS = ["z0", "z1", "ff0_0", "pw1_0", "ff0_1", "pw1_1", "ff1_0", "ff1_1"]
        PREP = {name: n for n, name in enumerate(PREPS)}
        STATS = ["z0", "z1", "ff0_0", "pw1_0", "ff0_1", "conv0", "pw1_1", "ff1_0", "conv1", "ff1_1"]
        STAT = {name: n for n, name in enumerate(STATS)}
        BCS = [s for s in STATS if s[0] != "z"]
        BC = {name: n for n, name in enumerate(BCS)}
        STAGE_OPERAND = {("ff0", 0): h_buf, ("pw1", 0): h_buf, ("ff0", 1): h_buf, ("pw1", 1): h_buf,
                         ("ff1", 0): h_buf, ("ff1", 1): hid_buf}

        def name_of(stage, half):
            return f"{stage}_{half}"

        @block.sync
        def _(sp):
            def unit(w, block_index, slot):
                if not isinstance(w, int) or w >= 2:
                    sp.wait_ge(lo_up, w - 1)
                sp.dma_start(raw[:, slot], weights[block_index]).then_inc(landed[slot], 16)

            for dst, src in ((gain[:], gains), (inv_f[:], inv_freq), (pos_i[:], positions),
                             (gh[:], g_head), (gvb[:], g_vb), (ws[:], w_s), (bs[:], b_s), (wdw[:], w_dw)):
                sp.dma_start(dst, src).then_inc(consts_in, 16)

            def x_tiles(half):
                for k in range(KT):
                    n = half * KT + k
                    if n >= 2:
                        sp.wait_ge(prep_lo, n - 1)
                        sp.wait_ge(prep_sq, n - 1)
                    sp.dma_start(x_in[:, k % 2], x_t[k, :, half * HALF:(half + 1) * HALF]
                                 ).then_inc(x_in_full[k % 2], 16)

            unit(0, 0, 0)
            unit(1, 1, 1)
            x_tiles(0)
            with sp.Fori(1, 8) as i:
                for r in range(2):
                    unit(2 * i + r, 2 * i + r, r)
            with sp.Fori(0, 2) as i:
                for r in range(2):
                    unit(16 + 2 * i + r, 2 * i + r, r)
            x_tiles(1)
            with sp.Fori(2, 8) as i:
                for r in range(2):
                    unit(16 + 2 * i + r, 2 * i + r, r)

            def stream(first, first_block, start, count):
                with sp.Fori(start // 2, count // 2) as i:
                    for r in range(2):
                        unit(32 + first + 2 * i + r, first_block + 2 * i + r, r)

            for name, half, first_block, count in STAGES:
                first = FIRST[name, half]
                if (name, half) == ("wout", 0):
                    stream(first, first_block, 0, 4)
                    sp.wait_ge(z_read, NSTEP)
                    sp.wait_ge(spat_used, 8)
                    sp.wait_ge(logit_used, LOGITS[8])
                    sp.wait_ge(tr_read, TR["q", 0, 0])
                    sp.dma_start(xt0[:], x_t[:, :, 0:HALF].rearrange("k p n -> p k n")).then_inc(x_full, 16)
                    stream(first, first_block, 4, count)
                    continue
                if (name, half) == ("wout", 1):
                    sp.wait_ge(q_split, 8)
                    sp.dma_start(xt1[:], x_t[:, :, HALF:SEQ].rearrange("k p n -> p k n")).then_inc(x_full, 16)
                stream(first, first_block, 0, count)
                if (name, half) == ("pw2", 1):
                    sp.wait_ge(unit_read, FIRST["ff1", 0] + 64)
                    sp.dma_start(out_t[:, :, 0:HALF].rearrange("k p n -> p k n"), xt0[:]).then_inc(out_sem, 16)
            for k in range(KT):
                sp.wait_ge(unit_read, NUNIT - KT + 1 + k)
                sp.dma_start(out_t[k, :, HALF:SEQ], xt1[:, k]).then_inc(out_sem, 16)
            sp.wait_ge(out_sem, 16 * (1 + KT))

        @block.tensor
        def _(pe):
            def products(acc, lhs_hi, lhs_lo, rhs_hi, rhs_lo, first, last):
                nc.tensor.matmul(acc, lhs_hi, rhs_hi, start=first, stop=False)
                nc.tensor.matmul(acc, lhs_hi, rhs_lo, start=False, stop=False)
                return nc.tensor.matmul(acc, lhs_lo, rhs_hi, start=False, stop=last)

            def sums_by_token(name, sums):
                n = STAT[name]
                for j in range(HT):
                    mm = nc.tensor.matmul(psum[:, 7, j:j + 1], sums[:, j * P:(j + 1) * P], ones[:, 0:1],
                                          start=True, stop=True)
                mm.then_inc(stat_up, 1)

            def broadcast_rms():
                mm = nc.tensor.matmul(psum[:, 7, :], ones[:], diag, start=True, stop=True)
                mm.then_inc(stat_bc, 1)

            def transpose_group(key, parts):
                n = TR[key]
                if n >= 3:
                    pe.wait_ge(tr_read, n - 2)
                    if key[0] in ("p", "q", "cat"):
                        done = [at for at in CATS if at <= n - 3]
                        if done:
                            pe.wait_ge(cat_lo, len(done))
                for dst, src in parts(psum[:, 4 + n % 3, :]):
                    tr = nc.tensor.transpose(dst, src, ident[:])
                tr.then_inc(tr_up, 1)

            pe.wait_ge(consts_up, CONSTS)

            def project(s):
                half, c, j = s // 16, s // 4 % 4, s % 4
                wb = (hid_buf, w_buf)[c % 2]
                n = CHUNK_COLS[c]
                if s >= 2:
                    pe.wait_ge(z_read, s - 1)
                if j == 0:
                    pe.wait_ge(lo_up, 4 * (s // 4 + 1))
                acc = psum[:, s % 2, 0:n]
                for k in range(KT):
                    if c == 0 and j == 0:
                        pe.wait_ge(prep_lo, half * KT + k + 1)
                    mm = products(acc, h_buf[:, 0, k, j * P:(j + 1) * P], h_buf[:, 1, k, j * P:(j + 1) * P],
                                  wb[:, 0, k, 0:n], wb[:, 1, k, 0:n], k == 0, k == KT - 1)
                mm.then_inc(z_up, 1)

            def turn_keys(t):
                pe.wait_ge(z_proc, 16 * (t // 4) + t % 4 + 1)
                transpose_group(("k", t, 0), lambda bank: [
                    (bank[:, 0:P], k_stack[:, 0:2, :].bitcast(F32).rearrange("p a d -> p (a d)")),
                    (bank[0:HD, P:2 * P], k_stack[:, 2, :].bitcast(F32)),
                    (bank[0:3 * ID, 2 * P:3 * P], ki_stack[:].bitcast(F32).rearrange("p a d -> p (a d)"))])
                if t >= 2:
                    for g in range(2):
                        transpose_group(("qi", t, g), lambda bank: [
                            (bank[0:3 * ID, i * P:(i + 1) * P],
                             qi_stack[:, 4 * g + i].bitcast(F32).rearrange("p a d -> p (a d)")) for i in range(4)])

            def index_logits(t):
                n = LOGITS[t]
                pe.wait_ge(tr_read, TR["qi", t, 1] + 1)
                for h in range(IH):
                    for c0 in range(0, P * (t + 1), HALF):
                        c1 = min(c0 + HALF, P * (t + 1))
                        if n >= 2:
                            pe.wait_ge(logit_relu, n - 1)
                        nc.tensor.matmul(psum[:, 2 + n % 2, 0:c1 - c0], qi_t[0:3 * ID, h, :], ki_t[0:3 * ID, c0:c1],
                                         start=True, stop=True).then_inc(logit_up, 1)
                        n += 1

            def spatial(t):
                pe.wait_ge(z_proc, 16 * (t // 4) + 12 + t % 4 + 1)
                if t >= 1:
                    pe.wait_ge(spat_used, t)
                for g in range(GROUPS):
                    mm = nc.tensor.matmul(psum[:, 7, g * GD:(g + 1) * GD], ws[:, g, :], qz[:, g * GD:(g + 1) * GD],
                                          start=True, stop=True)
                mm.then_inc(spat_up, 1)

            for s in range(NSTEP + 2):
                if s < NSTEP:
                    project(s)
                for back, job in ((1, turn_keys), (2, index_logits)):
                    b = s - back
                    if 0 <= b < NSTEP and b // 4 % 4 == KV:
                        t = b // 16 * 4 + b % 4
                        if job is turn_keys or t >= 2:
                            job(t)
                b = s - 1
                if 0 <= b < NSTEP and b // 4 % 4 == VC:
                    spatial(b // 16 * 4 + b % 4)
                if s in (0, 16):
                    pe.wait_ge(prep_sum, KT * (s // 16 + 1))
                    if s:
                        pe.wait_ge(spat_used, 4)
                    sums_by_token(f"z{s // 16}", sq_sum)

            def attention(half):
                pe.wait_ge(spat_used, 8)
                if half:
                    pe.wait_ge(unit_read, FIRST["pw1", 0])

                def cat(t):
                    pe.wait_ge(att_norm, t + 1)
                    for g, src in ((0, a_tok[:]), (1, b_tok[:, t, :])):
                        transpose_group(("cat", t, g), lambda bank: [
                            (bank[:, i * P:(i + 1) * P], src[:, i * P:(i + 1) * P]) for i in range(4)])

                def scores(t, h):
                    a = 8 * t + h
                    if a >= 2:
                        pe.wait_ge(qk_masked, a - 1)
                    for c0 in range(0, P * (t + 1), HALF):
                        c1 = min(c0 + HALF, P * (t + 1))
                        dst = psum[:, 2 * (a % 2) + c0 // HALF, 0:c1 - c0]
                        nc.tensor.matmul(dst, q_t[:, h, :], k_t[:, c0:c1], start=True, stop=False)
                        mm = nc.tensor.matmul(dst, q_t[0:HD, h, :], k_lo_t[:, c0:c1], start=False, stop=True)
                    mm.then_inc(qk_up, 1)

                def turn_probs(t, h):
                    a = 8 * t + h
                    pe.wait_ge(exp_up, a + 1)
                    for g in range((t + 4) // 4):
                        transpose_group(("p", t, h, g), lambda bank: [
                            (bank[:, (b % 4) * P:(b % 4 + 1) * P], p_buf[:, a % 2, b * P:(b + 1) * P])
                            for b in range(4 * g, min(4 * g + 4, t + 1))])

                def values(t, h):
                    a = 8 * t + h
                    pe.wait_ge(tr_read, TR["p", t, h, (t + 4) // 4 - 1] + 1)
                    if h == 0 and t % 4:
                        pe.wait_ge(att_norm, t)
                    for b in range(t + 1):
                        mm = nc.tensor.matmul(psum[:, 7, h * HD:(h + 1) * HD], pt_buf[:, a % 2, b * P:(b + 1) * P],
                                              v_tok[:, b, :], start=(b == 0), stop=(b == t))
                    mm.then_inc(pv_up, 1)

                for t in range(4 * half, 4 * half + 4):
                    pe.wait_ge(q_split, t + 1)
                    for g in range(2):
                        transpose_group(("q", t, g), lambda bank: [
                            (bank[:, i * P:(i + 1) * P],
                             q_stack[:, 4 * g + i].bitcast(F32).rearrange("p a d -> p (a d)")) for i in range(4)])
                    if t % 4:
                        cat(t - 1)
                    pe.wait_ge(tr_read, TR["q", t, 1] + 1)
                    for h in range(HEADS + 2):
                        if h < HEADS:
                            scores(t, h)
                        if 1 <= h <= HEADS:
                            turn_probs(t, h - 1)
                        if h >= 2:
                            values(t, h - 2)
                cat(4 * half + 3)

            def unit(m, slot, operand, ready=None, ready_at=0):
                pe.wait_ge(lo_up, 32 + m + 1)
                if not isinstance(m, int) or m >= 4:
                    pe.wait_ge(unit_read, m - 3)
                for k in range(KT):
                    if ready is not None:
                        pe.wait_ge(ready, ready_at + k + 1)
                    cols = slice(slot * P, (slot + 1) * P)
                    mm = products(psum[:, slot, :], w_buf[:, 0, k, cols], w_buf[:, 1, k, cols],
                                  operand[:, 0, k, :], operand[:, 1, k, :], k == 0, k == KT - 1)
                mm.then_inc(unit_up, 1)

            def units(first, count, operand, ready=None, ready_at=0, after=()):
                for r in range(4):
                    unit(first + r, r, operand, ready if r == 0 else None, ready_at)
                    for at, job in after:
                        if at == r:
                            job()
                if count > 4:
                    with pe.Fori(1, count // 4) as i:
                        for r in range(4):
                            unit(first + 4 * i + r, r, operand)

            def rms_jobs(name, prep):
                def take():
                    pe.wait_ge(prep_sum, KT * (PREP[prep] + 1))
                    sums_by_token(name, sq_sum)

                def spread():
                    pe.wait_ge(stat_diag, STAT[name] + 1)
                    broadcast_rms()
                return ((0, take), (2, spread))

            def mlp(stage, half, operand, hidden):
                first = FIRST[stage, half]
                name = name_of(stage, half)
                ups = UPS[stage, half]
                for q in range(4):
                    if q == 0:
                        units(first, 8, operand, prep_lo, KT * PREP[name], rms_jobs(name, name))
                    else:
                        units(first + 16 * q, 8, operand)
                        if q == 3 and (stage, half) in CONV_IN:
                            pe.wait_ge(stat_diag, STAT[CONV_IN[stage, half]] + 1)
                            broadcast_rms()
                    units(first + 16 * q + 8, 8, hidden, hid_lo, CREDIT + ups + 8 * q)
                    if q == 2 and (stage, half) in CONV_IN:
                        pe.wait_ge(conv_sum, CREDIT + 8 * (half == 0) + 8)
                        sums_by_token(CONV_IN[stage, half], c_sum)

            for name, half, _, count in STAGES:
                first = FIRST[name, half]
                if (name, half) == ("wout", 0):
                    attention(0)
                if (name, half) == ("pw1", 0):
                    attention(1)
                if name == "wout":
                    pe.wait_ge(cat_lo, 8 * (half + 1))
                    units(first, 8, hid_buf)
                elif name in ("ff0", "ff1"):
                    swapped = (name, half) == ("ff1", 1)
                    mlp(name, half, *((hid_buf, h_buf) if swapped else (h_buf, hid_buf)))
                elif name == "pw1":
                    n = name_of(name, half)
                    units(first, 16, h_buf, prep_lo, KT * PREP[n], rms_jobs(n, n))
                else:
                    units(first, 8, (hid_buf, h_buf)[half], act_lo, 8 * half)

        @block.gpsimd
        def _(pool):
            pool.sem_inc(hid_lo, CREDIT)
            pool.sem_inc(y_up, CREDIT)
            nc.gpsimd.memset(ident[:], 0.0).then_inc(pool_chain, 1)
            nc.gpsimd.memset(tri[:], 0.0).then_inc(pool_chain, 1)
            nc.gpsimd.memset(ones[:], 1.0).then_inc(consts_up, 1)
            pool.wait_ge(pool_chain, 2)
            nc.gpsimd.affine_select(out=ident[:], in_=ident[:], compare_op=ALU.not_equal, fill=1.0, base=0,
                                    pattern=[[-1, P]], channel_multiplier=1).then_inc(consts_up, 1)
            nc.gpsimd.affine_select(out=tri[:], in_=tri[:], compare_op=ALU.is_ge, fill=NEG, base=0,
                                    pattern=[[-1, P]], channel_multiplier=1).then_inc(consts_up, 1)
            pool.wait_ge(consts_in, 16 * 8)
            nc.gpsimd.affine_select(out=ws[:], in_=ws[:], compare_op=ALU.is_ge, fill=0.0, base=0,
                                    pattern=[[0, GROUPS], [1, P]], channel_multiplier=-1).then_inc(consts_up, 1)

            def split_lo(w, raw_slot, dst_hi, dst_lo):
                pool.wait_ge(hi_up, w + 1)
                nc.gpsimd.tensor_tensor(dst_lo, raw[:, raw_slot], dst_hi.bitcast(F32), ALU.subtract
                                        ).then_inc(lo_up, 1)

            for w in range(32):
                wb, cols = (hid_buf, w_buf)[w // 4 % 2], slice(w % 4 * P, (w % 4 + 1) * P)
                split_lo(w, w % 2, wb[:, 0, :, cols], wb[:, 1, :, cols])

            def split_main(m, slot):
                cols = slice(slot * P, (slot + 1) * P)
                split_lo(32 + m, slot % 2, w_buf[:, 0, :, cols], w_buf[:, 1, :, cols])

            for m in range(AHEAD):
                split_main(m, m)

            def units(first, count, job=None, last=False):
                def group(i):
                    for r in range(4):
                        if not (last and isinstance(i, int) and i == count // 4 - 1 and r >= 4 - AHEAD):
                            split_main(first + 4 * i + r + AHEAD, (r + AHEAD) % 4)
                        if job:
                            job(i, r)
                with pool.Fori(0, count // 4 - last) as i:
                    group(i)
                if last:
                    group(count // 4 - 1)

            def mlp(stage, half, hidden):
                first, ups = FIRST[stage, half], UPS[stage, half]
                for q in range(4):
                    def hidden_lo(i, r):
                        n = ups + 8 * q + 4 * i + r
                        pool.wait_ge(hid_hi, n + 1)
                        k = 4 * i + r
                        nc.gpsimd.tensor_tensor(flat(hidden, 1, k), s_ring[:, r % 2],
                                                flat(hidden, 0, k).bitcast(F32), ALU.subtract).then_inc(hid_lo, 1)

                    units(first + 16 * q, 8, hidden_lo)
                    job = None
                    if q == 3 and (stage, half) == ("ff1", 0):
                        job = swish_lo(1, h_buf)
                    units(first + 16 * q + 8, 8, job, last=(q == 3 and (stage, half) == ("ff1", 1)))

            def swish_lo(half, dst):
                def job(i, r, per=1):
                    n = 8 * half + 4 * i + r
                    k = 4 * i + r
                    pool.wait_ge(act_hi, n + 1)
                    nc.gpsimd.tensor_tensor(flat(dst, 1, k), s_ring[:, r % 2], flat(dst, 0, k).bitcast(F32),
                                            ALU.subtract).then_inc(act_lo, 1)
                return job

            for name, half, _, count in STAGES:
                first = FIRST[name, half]
                if name in ("ff0", "ff1"):
                    mlp(name, half, h_buf if (name, half) == ("ff1", 1) else hid_buf)
                elif name == "pw1":
                    if half == 0:
                        pool.wait_ge(cat_lo, 16)
                        pool.wait_ge(pv_up, 64)
                        nc.gpsimd.memset(y_buf[:, :, 0:CONV - 1], 0.0).then_inc(y_up, 1)
                    else:
                        pool.wait_ge(conv_step, CONV * KT)
                        nc.gpsimd.tensor_copy(y_buf[:, :, 0:CONV - 1], y_buf[:, :, HALF:HALF + CONV - 1]
                                              ).then_inc(y_up, 1)

                    def gated(i, r):
                        if r % 2:
                            n = 8 * half + 2 * i + r // 2
                            pool.wait_ge(gate_up, CREDIT + n + 1)
                            k = 2 * i + r // 2
                            if half:
                                pool.wait_ge(y_up, CREDIT + 10)
                            nc.gpsimd.tensor_tensor(yflat(k, CONV - 1), t_ring[:, r // 2], sq_ring[:, r // 2],
                                                    ALU.mult).then_inc(y_up, 1)
                    units(first, 16, gated)
                    if half:
                        job = swish_lo(0, hid_buf)
                        for k in range(KT):
                            job(k // 4, k % 4)
                else:
                    units(first, 8)

        @block.scalar
        def _(act):
            chain = [0]

            def link(ins):
                chain[0] += 1
                ins.then_inc(act_chain, 1)
                act.wait_ge(act_chain, chain[0])

            act.sem_inc(squared, CREDIT)
            act.sem_inc(gate_up, CREDIT)

            def prep(n0, k, src, dst, g, ready=None, ready_at=None):
                if ready is not None:
                    act.wait_ge(ready, ready_at)
                nc.scalar.activation(flat(dst, 0, k), src, ACT.Copy, scale=gflat(g, k)).then_inc(prep_hi, 1)

            def square(n0, k, ring, src):
                n = n0 + k
                if not isinstance(n, int) or n >= 2:
                    wait_apart(act, prep_sum, n - 1, passed_s)
                nc.scalar.activation(sq_ring[:, ring], src, ACT.Square).then_inc(prep_sq, 1)

            def split_hi(w, raw_slot, landings, dst):
                act.wait_ge(landed[raw_slot], 16 * landings)
                nc.scalar.activation(dst, raw[:, raw_slot], ACT.Copy).then_inc(hi_up, 1)

            def split_z(w):
                wb, cols = (hid_buf, w_buf)[w // 4 % 2], slice(w % 4 * P, (w % 4 + 1) * P)
                if w >= 8 and w % 4 == 0:
                    act.wait_ge(z_up, w - 4)
                split_hi(w, w % 2, w // 2 + 1, wb[:, 0, :, cols])

            act.wait_ge(consts_in, 16 * 8)
            act.wait_ge(rope_arg, 2)
            for dst in (sin, cos):
                nc.scalar.activation(dst[:], dst[:], ACT.Sin).then_inc(rope_up, 1)

            def prep_x(half):
                for k in range(KT):
                    if half and k == 0:
                        act.wait_ge(z_up, 16)
                        act.wait_ge(z_vsq, 4)
                    prep(KT * half, k, x_in[:, k % 2], h_buf, G_EV, x_in_full[k % 2],
                         16 * (half * 4 + k // 2 + 1))
                    square(KT * half, k, k % 2, x_in[:, k % 2])

            prep_x(0)
            for w in range(4):
                split_z(w)

            def evacuate(s):
                half, c, j = s // 16, s // 4 % 4, s % 4
                t = 4 * half + j
                src, r = psum[:, s % 2, 0:CHUNK_COLS[c]], r_tok[:, t:t + 1]
                act.wait_ge(z_up, s + 1)
                if s % 16 == 0:
                    act.wait_ge(stat_diag, half + 1)
                if c == KV:
                    if s:
                        act.wait_ge(z_proc, s)
                    nc.scalar.activation(zt[:], src, ACT.Copy, scale=r).then_inc(z_read, 1)
                elif c == QC:
                    act.wait_ge(z_proc, s)
                    if t == 4:
                        act.wait_ge(spat_up, 4)
                    nc.scalar.activation(qz[:], src, ACT.Copy, scale=r).then_inc(z_read, 1)
                elif c == UC:
                    nc.scalar.activation(b_tok[:, t, :], src, ACT.Gelu_apprx_tanh, scale=r).then_inc(z_read, 1)
                else:
                    if t:
                        act.wait_ge(spat_up, t)
                    act.wait_ge(z_proc, s)
                    nc.scalar.activation(qz[:], src, ACT.Gelu_apprx_tanh, scale=r).then_inc(z_read, 1)
                    act.wait_ge(z_read, s + 1)
                    nc.scalar.activation(sq_ring[:, 0], qz[:], ACT.Square, accum_out=vsum).then_inc(z_vsq, 1)

            def keys_out(t):
                act.wait_ge(tr_up, TR["k", t, 0] + 1)
                bank, cols = psum[:, 4 + TR["k", t, 0] % 3, :], slice(t * P, (t + 1) * P)
                nc.scalar.copy(k_t[:, cols], bank[:, 0:P])
                nc.scalar.copy(k_lo_t[:, cols], bank[0:HD, P:2 * P])
                nc.scalar.copy(ki_t[0:3 * ID, cols], bank[0:3 * ID, 2 * P:3 * P]).then_inc(tr_read, 1)
                if t >= 2:
                    for g in range(2):
                        n = TR["qi", t, g]
                        act.wait_ge(tr_up, n + 1)
                        if t > 2:
                            act.wait_ge(logit_up, LOGITS[t])
                        nc.scalar.copy(qi_t[0:3 * ID, 4 * g:4 * g + 4, :].rearrange("p h n -> p (h n)"),
                                       psum[0:3 * ID, 4 + n % 3, :]).then_inc(tr_read, 1)

            def relus(t, s):
                act.wait_ge(z_proc, s)
                n = LOGITS[t]
                for h in range(IH):
                    for c0 in range(0, P * (t + 1), HALF):
                        c1 = min(c0 + HALF, P * (t + 1))
                        act.wait_ge(logit_up, n + 1)
                        if n >= 2:
                            act.wait_ge(logit_used, n - 1)
                        nc.scalar.activation(tmp[:, n % 2, 0:c1 - c0], psum[:, 2 + n % 2, 0:c1 - c0], ACT.Relu
                                             ).then_inc(logit_relu, 1)
                        n += 1

            for s in range(NSTEP + 2):
                if s == 16:
                    prep_x(1)
                if s < 28:
                    split_z(s + 4)
                if s < NSTEP:
                    evacuate(s)
                for back in (2, 1):
                    b = s - back
                    if 0 <= b < NSTEP and b // 4 % 4 == KV:
                        t = b // 16 * 4 + b % 4
                        if back == 1:
                            keys_out(t)
                        elif t >= 2:
                            relus(t, min(s + 1, NSTEP))

            def split_main(m, slot, landings):
                if not isinstance(m, int) or m >= 4:
                    act.wait_ge(unit_up, m - 3)
                if isinstance(m, int) and m < 4:
                    act.wait_ge(z_up, NSTEP)
                split_hi(32 + m, slot % 2, landings, w_buf[:, 0, :, slot * P:(slot + 1) * P])

            for m in range(AHEAD):
                split_main(m, m, 16 + m // 2 + 1)

            def attention(half):
                def bank_out(key, dst, rows=slice(0, P), cols=HALF):
                    n = TR[key]
                    act.wait_ge(tr_up, n + 1)
                    return nc.scalar.copy(dst, psum[rows, 4 + n % 3, 0:cols])

                def cat(t):
                    j = t % 4
                    for g in range(2):
                        n = TR["cat", t, g]
                        act.wait_ge(tr_up, n + 1)
                        nc.scalar.copy(hid_buf[:, 0, 4 * g:4 * g + 4, j * P:(j + 1) * P],
                                       psum[:, 4 + n % 3, :].rearrange("p (k n) -> p k n", k=4)).then_inc(cat_hi, 1)
                        act.wait_ge(cat_hi, 2 * t + g + 1)
                        act.sem_inc(tr_read, 1)

                if half == 0:
                    act.wait_ge(z_up, NSTEP)
                for t in range(4 * half, 4 * half + 4):
                    for g in range(2):
                        if t % 4 and g == 0:
                            act.wait_ge(qk_up, 8 * t)
                        bank_out(("q", t, g), q_t[:, 4 * g:4 * g + 4, :].rearrange("p h n -> p (h n)")
                                 ).then_inc(tr_read, 1)
                    if t % 4:
                        cat(t - 1)
                        act.wait_ge(att_norm, t)
                    n = P * (t + 1)
                    for h in range(HEADS + 1):
                        a = 8 * t + h
                        if h < HEADS:
                            act.wait_ge(neg_up, a + 1)
                            if a >= 2 and h >= 2:
                                act.wait_ge(tr_up, TR["p", t, h - 2, (t + 4) // 4 - 1] + 1)
                            nc.scalar.activation(p_buf[:, a % 2, 0:n], s_buf[:, a % 2, 0:n], ACT.Exp,
                                                 bias=neg_max[:, a % 2:a % 2 + 1], scale=HD ** -0.5,
                                                 accum_out=row_sum[:, h:h + 1]).then_inc(exp_up, 1)
                        if h >= 1:
                            b = a - 1
                            if b >= 2:
                                act.wait_ge(pv_up, b - 1)
                            for g in range((t + 4) // 4):
                                cols = min(HALF, n - g * HALF)
                                bank_out(("p", t, h - 1, g), pt_buf[:, b % 2, g * HALF:g * HALF + cols], cols=cols
                                         ).then_inc(tr_read, 1)
                cat(4 * half + 3)

            def units(first, count, job=None, last=False):
                def group(i):
                    for r in range(4):
                        if not (last and isinstance(i, int) and i == count // 4 - 1 and r >= 4 - AHEAD):
                            split_main(first + 4 * i + r + AHEAD, (r + AHEAD) % 4,
                                       16 + first // 2 + 2 * i + (r + AHEAD) // 2 + 1)
                        if job:
                            job(i, r)
                if first == 0:
                    for i in range(count // 4):
                        group(i)
                    return
                with act.Fori(0, count // 4 - last) as i:
                    group(i)
                if last:
                    group(count // 4 - 1)

            def final(first, half, name, g, dst):
                n0 = KT * PREP[name]

                def job(i, r):
                    k = 4 * i + r
                    wait_apart(act, unit_read, first + 4 * i + r + 1, passed_s)
                    prep(n0, k, flat(xt[half], None, k), dst, g)
                    square(n0, k, r % 2, flat(xt[half], None, k))
                return job

            def swish(half, dst):
                def job(i, r):
                    k = 4 * i + r
                    n = 8 * half + k
                    act.wait_ge(act_in, n + 1)
                    if not isinstance(n, int) or n >= 2:
                        act.wait_ge(act_lo, n - 1)
                    nc.scalar.activation(s_ring[:, r % 2], t_ring[:, r % 2], ACT.Silu).then_inc(act_silu, 1)
                    wait_apart(act, act_silu, n + 1, passed_s)
                    nc.scalar.activation(flat(dst, 0, k), s_ring[:, r % 2], ACT.Copy).then_inc(act_hi, 1)
                return job

            def both(*jobs):
                def job(i, r):
                    for j in jobs:
                        if j:
                            j(i, r)
                return job

            def mlp(stage, half, hidden, following):
                first, ups = FIRST[stage, half], UPS[stage, half]
                conv = (stage, half) in CONV_IN
                for q in range(4):
                    def hidden_hi(i, r):
                        k = 4 * i + r
                        n = ups + 8 * q + k
                        act.wait_ge(unit_read, first + 16 * q + k + 1)
                        act.wait_ge(hid_lo, CREDIT + n - 1)
                        nc.scalar.activation(s_ring[:, r % 2], t_ring[:, r % 2], ACT.Square).then_inc(squared, 1)
                        wait_apart(act, squared, CREDIT + n + 1, passed_s)
                        nc.scalar.activation(flat(hidden, 0, k), s_ring[:, r % 2], ACT.Copy).then_inc(hid_hi, 1)

                    def conv_squares(i, r):
                        k = 4 * i + r
                        n = 8 * (half == 0) + k
                        act.wait_ge(conv_step, CONV * KT * (1 + (half == 0)))
                        act.wait_ge(hid_lo, CREDIT + ups + 24)
                        act.wait_ge(conv_sum, CREDIT + n - 1)
                        nc.scalar.activation(s_ring[:, r % 2], flat(c_buf, None, k), ACT.Square).then_inc(conv_sq, 1)

                    units(first + 16 * q, 8, hidden_hi)
                    job = None
                    if conv and q == 2:
                        job = conv_squares
                    if q == 3:
                        down = first + 16 * q + 8
                        job = both(final(down, half, *following) if following else None,
                                   swish(1, h_buf) if (stage, half) == ("ff1", 0) else None)
                    units(first + 16 * q + 8, 8, job, last=(q == 3 and (stage, half) == ("ff1", 1)))

            for name, half, _, count in STAGES:
                first = FIRST[name, half]
                if (name, half) == ("wout", 0):
                    attention(0)
                if (name, half) == ("pw1", 0):
                    attention(1)
                    act.wait_ge(unit_read, first)
                    for k in range(KT):
                        prep(KT * PREP["pw1_0"], k, xt0[:, k], h_buf, G_OD)
                        square(KT * PREP["pw1_0"], k, k % 2, xt0[:, k])
                if name == "wout":
                    if half:
                        act.wait_ge(y_up, CREDIT + 9)
                    units(first, 8, final(first, half, f"ff0_{half}", G_FF0, h_buf))
                elif name == "pw2":
                    act.wait_ge(y_up, CREDIT + 18)
                    units(first, 8, final(first, half, f"ff1_{half}", G_FF1, (h_buf, hid_buf)[half]))
                elif name == "pw1":
                    def gate(i, r):
                        if r % 2:
                            n = 8 * half + 2 * i + r // 2
                            act.wait_ge(unit_read, first + 4 * i + r + 1)
                            act.wait_ge(y_up, CREDIT + n + half)
                            nc.scalar.activation(sq_ring[:, r // 2], s_ring[:, r // 2], ACT.Sigmoid
                                                 ).then_inc(gate_up, 1)
                    units(first, 16, gate)
                    if half:
                        act.wait_ge(gate_up, CREDIT + 16)
                        job = swish(0, hid_buf)
                        for k in range(KT):
                            job(k // 4, k % 4)
                else:
                    if name == "ff1":
                        act.wait_ge(act_lo, 8 * (half + 1))
                    mlp(name, half, h_buf if (name, half) == ("ff1", 1) else hid_buf,
                        {("ff0", 1): ("pw1_1", G_OD, h_buf)}.get((name, half)))

        @block.vector
        def _(dve):
            V = nc.vector
            chain = [0]

            def link(ins):
                chain[0] += 1
                ins.then_inc(dve_chain, 1)
                dve.wait_ge(dve_chain, chain[0])

            def rsqrt(dst, v, n):
                y, a = st_y[:, 0:n], st_a[:, 0:n]
                link(V.tensor_scalar(y.bitcast(I32), v.bitcast(I32), 1, None, ALU.logical_shift_right))
                link(V.tensor_scalar(y.bitcast(I32), y.bitcast(I32), -1.0, float(0x5F3759DF), ALU.mult, ALU.add))
                for step in range(3):
                    link(V.tensor_tensor(a, y, y, ALU.mult))
                    link(V.scalar_tensor_tensor(out=a, in0=a, scalar=-0.5, in1=v, op0=ALU.mult, op1=ALU.mult))
                    link(V.scalar_tensor_tensor(out=dst if step == 2 else y, in0=a, scalar=1.5, in1=y,
                                                op0=ALU.add, op1=ALU.mult))

            def rms_of(name, dst):
                dve.wait_ge(stat_up, STAT[name] + 1)
                link(V.tensor_scalar(st_v[:, 0:HT], psum[:, 7, 0:HT], 1.0 / D, EPS, ALU.mult, ALU.add))
                rsqrt(dst, st_v[:, 0:HT], HT)

            def rms_diag(name):
                rms_of(name, r_inv[:, 0:HT])
                for j in range(HT):
                    ins = V.tensor_scalar(diag[:, j * P:(j + 1) * P], ident[:], r_inv[:, j:j + 1], None, ALU.mult)
                    if j < HT - 1:
                        link(ins)
                ins.then_inc(stat_diag, 1)

            def rms_spread(name, dst):
                dve.wait_ge(stat_bc, BC[name] + 1)
                link(V.tensor_copy(dst[:], psum[:, 7, :]))

            def clear_sum():
                link(V.memset(sq_sum[:], 0.0))

            def prep(n0, k, ring, src, dst, g):
                n = n0 + k
                dve.wait_ge(prep_hi, n + 1)
                V.scalar_tensor_tensor(out=flat(dst, 1, k), in0=src, scalar=gflat(g, k),
                                       in1=flat(dst, 0, k).bitcast(F32), op0=ALU.mult, op1=ALU.subtract
                                       ).then_inc(prep_lo, 1)
                dve.wait_ge(prep_sq, n + 1)
                if not isinstance(n, int) or n >= 1:
                    dve.wait_ge(prep_sum, n)
                V.tensor_tensor(sq_sum[:], sq_sum[:], sq_ring[:, ring], ALU.add).then_inc(prep_sum, 1)

            dve.sem_inc(conv_sum, CREDIT)
            dve.wait_ge(consts_in, 16 * 8)
            dve.wait_ge(consts_up, CONSTS)
            link(V.tensor_copy(pos_f, pos_i[:]))
            ang, turns = qz[:, 0:256].rearrange("p (t f) -> p t f", t=8), qz[:, 256:512].rearrange("p (t f) -> p t f", t=8)
            for t in range(8):
                link(V.tensor_scalar(ang[:, t], inv_f[:], pos_f[:, t:t + 1], None, ALU.mult))
            TWO_PI = 2 * np.pi
            C1 = 6.28125
            C2 = float(np.float32(np.round((TWO_PI - C1) * 2 ** 19) / 2 ** 19))
            C3 = float(np.float32(TWO_PI - C1 - C2))
            MAGIC = 1.5 * 2 ** 23
            for dst, shift in ((sin, 0.0), (cos, 0.25)):
                link(V.tensor_scalar(turns, ang, float(1 / TWO_PI), shift, ALU.mult, ALU.add))
                link(V.tensor_scalar(turns, turns, MAGIC, None, ALU.add))
                link(V.tensor_scalar(turns, turns, MAGIC, None, ALU.subtract))
                link(V.scalar_tensor_tensor(out=dst[:], in0=turns, scalar=-C1, in1=ang, op0=ALU.mult, op1=ALU.add))
                link(V.scalar_tensor_tensor(out=dst[:], in0=turns, scalar=-C2, in1=dst[:], op0=ALU.mult, op1=ALU.add))
                link(V.scalar_tensor_tensor(out=dst[:], in0=turns, scalar=-C3, in1=dst[:], op0=ALU.mult, op1=ALU.add))
                if shift:
                    link(V.tensor_scalar(dst[:], dst[:], float(np.pi / 2), None, ALU.add))
                V.tensor_scalar(dst[:], dst[:], 3.1415925, -3.1415925, ALU.min, ALU.max).then_inc(rope_arg, 1)

            def prep_x(half):
                clear_sum()
                for k in range(KT):
                    prep(KT * half, k, k % 2, x_in[:, k % 2], h_buf, G_EV)

            def rms_x(half):
                rms_of(f"z{half}", r_tok[:, 4 * half:4 * half + 4])
                dve.sem_inc(stat_diag, 1)

            def rope(dst, src, t, heads, d):
                h = d // 2
                c = cos[:, t, ::HD // d][:, None, :].broadcast_to([P, heads, h])
                s = sin[:, t, ::HD // d][:, None, :].broadcast_to([P, heads, h])
                other = tmp[:, 1, 0:heads * d].rearrange("p (n d) -> p n d", d=d)
                V.tensor_tensor(dst[:, :, 0:h], src[:, :, 0:h], c, ALU.mult)
                V.tensor_tensor(dst[:, :, h:d], src[:, :, h:d], c, ALU.mult)
                V.tensor_tensor(other[:, :, 0:h], src[:, :, h:d], s, ALU.mult)
                link(V.tensor_tensor(other[:, :, h:d], src[:, :, 0:h], s, ALU.mult))
                V.tensor_tensor(dst[:, :, 0:h], dst[:, :, 0:h], other[:, :, 0:h], ALU.subtract)
                link(V.tensor_tensor(dst[:, :, h:d], dst[:, :, h:d], other[:, :, h:d], ALU.add))

            def mean_square(dst, src, n):
                link(V.tensor_tensor_reduce(out=tmp[:, 1, 0:n], in0=src, in1=src, scale=1.0 / n, scalar=EPS,
                                            op0=ALU.mult, op1=ALU.add, accum_out=dst))

            def process_keys(s, t):
                dve.wait_ge(z_read, s + 1)
                if t >= 1:
                    dve.wait_ge(tr_up, TR["k", t - 1, 0] + 1 + 2 * (t - 1 >= 2))
                V.tensor_copy(v_tok[:, t, :], zt[:, V0:V0 + HD])
                link(V.tensor_scalar(w_idx[t % 3], zt[:, WI0:WI0 + IH], IDX_SCALE, None, ALU.mult))
                mean_square(st_v[:, 0:1], zt[:, K0:K0 + HD], HD)
                mean_square(st_v[:, 1:2], zt[:, KI0:KI0 + ID], ID)
                rsqrt(r_inv[:, 0:2], st_v[:, 0:2], 2)
                kn, kin = zt[:, K0:K0 + HD], zt[:, KI0:KI0 + ID]
                link(V.scalar_tensor_tensor(out=kn, in0=kn, scalar=r_inv[:, 0:1], in1=gh[:, 1, :],
                                            op0=ALU.mult, op1=ALU.mult))
                link(V.scalar_tensor_tensor(out=kin, in0=kin, scalar=r_inv[:, 1:2], in1=gh[:, 2, 0:ID],
                                            op0=ALU.mult, op1=ALU.mult))
                if s == 0:
                    dve.wait_ge(rope_up, 2)
                kr = tmp[:, 0, 0:HD]
                rope(kr.rearrange("p (n d) -> p n d", n=1), kn.rearrange("p (n d) -> p n d", n=1), t, 1, HD)
                link(V.tensor_copy(k_stack[:, 0:2, :], kr[:, None, :].broadcast_to([P, 2, HD])))
                link(V.tensor_tensor(k_stack[:, 2, :], kr, k_stack[:, 0, :].bitcast(F32), ALU.subtract))
                kr = tmp[:, 0, HD:HD + ID]
                rope(kr.rearrange("p (n d) -> p n d", n=1), kin.rearrange("p (n d) -> p n d", n=1), t, 1, ID)
                link(V.tensor_copy(ki_stack[:, 0:2, :], kr[:, None, :].broadcast_to([P, 2, ID])))
                ins = V.tensor_tensor(ki_stack[:, 2, :], kr, ki_stack[:, 0, :].bitcast(F32), ALU.subtract)
                if t >= 2:
                    link(ins)
                    qr = tmp[:, 0, 0:IH * ID].rearrange("p (n d) -> p n d", n=IH)
                    rope(qr, zt[:, QI0:KI0].rearrange("p (n d) -> p n d", n=IH), t, IH, ID)
                    link(V.tensor_copy(qi_stack[:, :, 0, :], qr))
                    V.tensor_copy(qi_stack[:, :, 2, :], qr)
                    ins = V.tensor_tensor(qi_stack[:, :, 1, :], qr, qi_stack[:, :, 0, :].bitcast(F32), ALU.subtract)
                ins.then_inc(z_proc, 1)

            def process_queries(s, t):
                dve.wait_ge(z_read, s + 1)
                heads = qz[:].rearrange("p (n d) -> p n d", n=HEADS)
                squares = tmp[:, 0].rearrange("p (n d) -> p n d", n=HEADS)
                link(V.tensor_tensor(squares, heads, heads, ALU.mult))
                link(V.tensor_reduce(st_v[:, 0:HEADS], squares, AX_X, ALU.add))
                link(V.tensor_scalar(st_v[:, 0:HEADS], st_v[:, 0:HEADS], 1.0 / HD, EPS, ALU.mult, ALU.add))
                rsqrt(r_inv[:, 0:HEADS], st_v[:, 0:HEADS], HEADS)
                link(V.tensor_tensor(squares, heads, r_inv[:, 0:HEADS][:, :, None].broadcast_to([P, HEADS, HD]), ALU.mult))
                link(V.tensor_tensor(squares, squares, gh[:, 0, :][:, None, :].broadcast_to([P, HEADS, HD]), ALU.mult))
                rope(q_tok[:, t], squares, t, HEADS, HD)
                dve.sem_inc(z_proc, 1)

            def process_v(s, t):
                dve.wait_ge(z_vsq, t + 1)
                link(V.tensor_scalar(st_v[:, 0:1], vsum, 1.0 / HALF, EPS, ALU.mult, ALU.add))
                rsqrt(r_inv[:, 0:1], st_v[:, 0:1], 1)
                V.scalar_tensor_tensor(out=qz[:], in0=qz[:], scalar=r_inv[:, 0:1], in1=gvb[:],
                                       op0=ALU.mult, op1=ALU.mult).then_inc(z_proc, 1)

            def gate_v(t):
                dve.wait_ge(spat_up, t + 1)
                groups = psum[:, 7, :].rearrange("p (g d) -> p g d", g=GROUPS)
                link(V.tensor_tensor(tmp[:, 0].rearrange("p (g d) -> p g d", g=GROUPS), groups,
                                     bs[:][:, :, None].broadcast_to([P, GROUPS, GD]), ALU.add))
                V.tensor_tensor(b_tok[:, t, :], b_tok[:, t, :], tmp[:, 0], ALU.mult).then_inc(spat_used, 1)

            def index_scores(t):
                n = LOGITS[t]
                for h in range(IH):
                    for c0 in range(0, P * (t + 1), HALF):
                        c1 = min(c0 + HALF, P * (t + 1))
                        dve.wait_ge(logit_relu, n + 1)
                        dst, src, w = score[t][:, c0:c1], tmp[:, n % 2, 0:c1 - c0], w_idx[t % 3][:, h:h + 1]
                        if h == 0:
                            ins = V.tensor_scalar(dst, src, w, None, ALU.mult)
                        else:
                            back = 1 if c1 == P * (t + 1) and c0 == 0 else 2
                            dve.wait_ge(logit_used, n + 1 - back)
                            ins = V.scalar_tensor_tensor(out=dst, in0=src, scalar=w, in1=dst,
                                                         op0=ALU.mult, op1=ALU.add)
                        ins.then_inc(logit_used, 1)
                        n += 1
                dve.wait_ge(logit_used, n)
                last = score[t][:, P * t:P * (t + 1)]
                link(V.tensor_tensor(last, last, tri[:], ALU.add))

            def topk(t, at):
                V.max(top8, score[t][:]).then_inc(topk_step, 1)
                wait_apart(dve, topk_step, 2 * at + 1, passed_v)
                V.match_replace(out=score[t][:], in_to_replace=top8, in_values=score[t][:], imm_value=TAKEN
                                ).then_inc(topk_step, 1)
                wait_apart(dve, topk_step, 2 * at + 2, passed_v)

            prep_x(0)
            rms_x(0)
            for s in range(NSTEP + 2):
                if s == 16:
                    prep_x(1)
                    gate_v(3)
                    rms_x(1)
                c, t = s // 4 % 4, s // 16 * 4 + s % 4
                if s < NSTEP:
                    if c == KV:
                        process_keys(s, t)
                    elif c == QC:
                        process_queries(s, t)
                    elif c == UC:
                        dve.wait_ge(z_read, s + 1)
                        dve.sem_inc(z_proc, 1)
                    else:
                        process_v(s, t)
                b = s - 2
                if 0 <= b and b // 4 % 4 == KV and b // 16 * 4 + b % 4 >= 2:
                    index_scores(b // 16 * 4 + b % 4)
                b = s - 1
                if 0 <= b < NSTEP and b // 4 % 4 == VC and b != 15:
                    gate_v(b // 16 * 4 + b % 4)
                if 8 <= s < 16:
                    with dve.Fori(0, 8) as i:
                        topk(2 + (s >= 12), (s - 8) * 8 + i)

            def attention(half):
                def cat(t):
                    j = t % 4
                    for g in range(2):
                        n = TR["cat", t, g]
                        dve.wait_ge(cat_hi, 2 * t + g + 1)
                        cols = slice(j * P, (j + 1) * P)
                        V.tensor_tensor(hid_buf[:, 1, 4 * g:4 * g + 4, cols],
                                        psum[:, 4 + n % 3, :].rearrange("p (k n) -> p k n", k=4),
                                        hid_buf[:, 0, 4 * g:4 * g + 4, cols].bitcast(F32), ALU.subtract
                                        ).then_inc(cat_lo, 1)

                def normalise(t):
                    dve.wait_ge(exp_up, 8 * t + 8)
                    link(V.reciprocal(r_inv, row_sum))
                    dve.wait_ge(pv_up, 8 * t + 8)
                    V.tensor_tensor(a_tok[:].rearrange("p (n d) -> p n d", n=HEADS),
                                    psum[:, 7, :].rearrange("p (n d) -> p n d", n=HEADS),
                                    r_inv[:, :, None].broadcast_to([P, HEADS, HD]), ALU.mult).then_inc(att_norm, 1)

                dve.wait_ge(z_up, NSTEP)
                for t in range(4 * half, 4 * half + 4):
                    if t % 4:
                        if t % 4 >= 2:
                            dve.wait_ge(cat_hi, 2 * (t - 1))
                        normalise(t - 1)
                    if t % 4:
                        dve.wait_ge(tr_up, TR["q", t - 1, 1] + 1)
                    link(V.tensor_copy(q_stack[:, :, 0, :], q_tok[:, t]))
                    V.tensor_tensor(q_stack[:, :, 1, :], q_tok[:, t], q_stack[:, :, 0, :].bitcast(F32), ALU.subtract
                                    ).then_inc(q_split, 1)
                    if t >= 2:
                        link(V.tensor_scalar(score[t][:], score[t][:], 0.9 * TAKEN, NEG, ALU.is_gt, ALU.mult))
                    if t % 4:
                        cat(t - 1)
                    n = P * (t + 1)
                    for h in range(HEADS):
                        a = 8 * t + h
                        dve.wait_ge(qk_up, a + 1)
                        if a >= 2:
                            dve.wait_ge(exp_up, a - 1)
                        logits = psum[:, 2 * (a % 2):2 * (a % 2) + 2, :].rearrange("p b n -> p (b n)")
                        s, m = s_buf[:, a % 2], row_max[:, a % 2:a % 2 + 1]
                        if t >= 2:
                            V.tensor_tensor_reduce(out=s[:, 0:n], in0=logits[:, 0:n], in1=score[t][:], scale=1.0,
                                                   scalar=NEG, op0=ALU.add, op1=ALU.max, accum_out=m
                                                   ).then_inc(qk_masked, 1)
                        else:
                            if t == 1:
                                link(V.tensor_copy(s[:, 0:P], logits[:, 0:P]))
                            link(V.tensor_tensor(s[:, n - P:n], logits[:, n - P:n], tri[:], ALU.add))
                            V.tensor_reduce(m, s[:, 0:n], AX_X, ALU.max).then_inc(qk_masked, 1)
                        dve.wait_ge(qk_masked, a + 1)
                        V.tensor_scalar(neg_max[:, a % 2:a % 2 + 1], m, -(HD ** -0.5), None, ALU.mult
                                        ).then_inc(neg_up, 1)
                t = 4 * half + 3
                dve.wait_ge(cat_hi, 2 * t)
                normalise(t)
                cat(t)

            def units(first, count, *jobs):
                with dve.Fori(0, count // 4) as i:
                    for r in range(4):
                        for job in jobs:
                            if job:
                                job(i, r)

            def add_residual(first, half):
                def job(i, r):
                    m = first + 4 * i + r
                    x = flat(xt[half], None, 4 * i + r)
                    dve.wait_ge(unit_up, m + 1)
                    if first >= 2 * KT:
                        dve.wait_ge(unit_read, m - KT)
                    V.tensor_tensor(x, x, psum[:, r, :], ALU.add).then_inc(unit_read, 1)
                return job

            def final(half, name, g, dst):
                n0 = KT * PREP[name]

                def job(i, r):
                    prep(n0, 4 * i + r, r % 2, flat(xt[half], None, 4 * i + r), dst, g)
                return job

            def convolve(half, q, part):
                def job(i, r):
                    ct = 4 * q + 2 * part + i
                    dst = flat(c_buf, None, ct)
                    for k in range(8 * r, min(8 * r + 8, CONV)):
                        n = CONV * (KT * half + 4 * q + 2 * part + i) + k
                        w = wdw[:, ct, k:k + 1]
                        src = yflat(ct, k)
                        if k == 0:
                            V.tensor_scalar(dst, src, w, gflat(B_DW, ct), ALU.mult, ALU.add).then_inc(conv_step, 1)
                        else:
                            dve.wait_ge(conv_step, n)
                            V.scalar_tensor_tensor(out=dst, in0=src, scalar=w, in1=dst, op0=ALU.mult, op1=ALU.add
                                                   ).then_inc(conv_step, 1)
                return job

            def conv_squares(half):
                def job(i, r):
                    n = 8 * half + 4 * i + r
                    dve.wait_ge(conv_sq, n + 1)
                    dve.wait_ge(conv_sum, CREDIT + n)
                    V.tensor_tensor(c_sum[:], c_sum[:], s_ring[:, r % 2], ALU.add).then_inc(conv_sum, 1)
                return job

            def swish_arg(half):
                def job(i, r):
                    k = 4 * i + r
                    n = 8 * half + k
                    if half or k >= 2:
                        dve.wait_ge(act_silu, n - 1)
                    V.scalar_tensor_tensor(out=t_ring[:, r % 2], in0=flat(c_buf, None, k), scalar=gflat(G_CONV, k),
                                           in1=conv_bc[:], op0=ALU.mult, op1=ALU.mult).then_inc(act_in, 1)
                return job

            def mlp(stage, half, following):
                first, ups = FIRST[stage, half], UPS[stage, half]
                name = name_of(stage, half)
                conv = CONV_IN.get((stage, half))
                conv_half = int(half == 0)
                rms_diag(name)
                rms_spread(name, rms_bc)
                if (stage, half) == ("ff0", 1):
                    dve.wait_ge(y_up, CREDIT + 9)
                if conv:
                    dve.wait_ge(y_up, CREDIT + 9 * (conv_half + 1))
                for q in range(4):
                    up, down = first + 16 * q, first + 16 * q + 8

                    def relu_scaled(i, r):
                        k = 4 * i + r
                        n = ups + 8 * q + k
                        dve.wait_ge(unit_up, up + k + 1)
                        dve.wait_ge(squared, CREDIT + n - 1)
                        V.scalar_tensor_tensor(out=t_ring[:, r % 2], in0=psum[:, r, :], scalar=0.0, in1=rms_bc[:],
                                               op0=ALU.max, op1=ALU.mult).then_inc(unit_read, 1)

                    def more_topk(part):
                        def job(i, r):
                            t = 4 + q
                            for z in range(2):
                                topk(t, 2 * ROUNDS + ROUNDS * q + 16 * part + 8 * i + 2 * r + z)
                        return job if (stage, half) == ("ff0", 0) else None

                    if conv and q == 2:
                        link(V.memset(c_sum[:], 0.0))
                    if conv and q == 3:
                        rms_diag(conv)
                    if conv and q < 2:
                        units(up, 8, relu_scaled, convolve(conv_half, q, 0))
                        units(down, 8, add_residual(down, half), convolve(conv_half, q, 1))
                        continue
                    units(up, 8, relu_scaled, more_topk(0))
                    if q == 3:
                        if conv:
                            rms_spread(conv, conv_bc)
                        if following:
                            clear_sum()
                        units(down, 8, add_residual(down, half), final(half, *following) if following else None,
                              swish_arg(1) if (stage, half) == ("ff1", 0) else None, more_topk(1))
                    else:
                        units(down, 8, add_residual(down, half), more_topk(1),
                              conv_squares(conv_half) if conv and q == 2 else None)

            for name, half, _, count in STAGES:
                first = FIRST[name, half]
                if (name, half) == ("wout", 0):
                    attention(0)
                    dve.wait_ge(x_full, 16)
                if (name, half) == ("pw1", 0):
                    attention(1)
                    clear_sum()
                    for k in range(KT):
                        prep(KT * PREP["pw1_0"], k, k % 2, xt0[:, k], h_buf, G_OD)
                if name == "wout":
                    if half:
                        dve.wait_ge(x_full, 32)
                    clear_sum()
                    units(first, 8, add_residual(first, half), final(half, f"ff0_{half}", G_FF0, h_buf))
                elif name == "pw2":
                    clear_sum()
                    units(first, 8, add_residual(first, half),
                          final(half, f"ff1_{half}", G_FF1, (h_buf, hid_buf)[half]))
                elif name == "pw1":
                    rms_diag(f"pw1_{half}")
                    rms_spread(f"pw1_{half}", rms_bc)

                    def scale_pair(i, r):
                        p = 8 * half + 2 * i + r // 2
                        dve.wait_ge(unit_up, first + 4 * i + r + 1)
                        if r % 2 == 0:
                            dve.wait_ge(y_up, CREDIT + p + half)
                            dst = t_ring
                        else:
                            dve.wait_ge(gate_up, CREDIT + p - 1)
                            dst = s_ring
                        V.tensor_tensor(dst[:, r // 2], psum[:, r, :], rms_bc[:], ALU.mult).then_inc(unit_read, 1)
                    units(first, 16, scale_pair)
                    if half:
                        dve.wait_ge(y_up, CREDIT + 18)
                        job = swish_arg(0)
                        for k in range(KT):
                            job(k // 4, k % 4)
                else:
                    mlp(name, half, {("ff0", 1): ("pw1_1", G_OD, h_buf)}.get((name, half)))


def kernel(**inputs):
    import concourse.bacc as bacc
    from concourse.bass_utils import run_bass_kernel_spmd

    x = np.asarray(inputs["x"])
    w_in = np.asarray(inputs["ev_w_in"])[0]

    def units_of(w):
        rows, cols = w.shape
        return w.reshape(rows // D, KT, P, cols // P, P).transpose(0, 3, 2, 1, 4)

    q, kvi, u, v = (w_in[:, 0:512], w_in[:, 512:936], w_in[:, 936:1448], w_in[:, 1448:1960])
    kvi = np.concatenate([kvi, np.zeros((D, 512 - C0), w_in.dtype)], axis=1)
    z_blocks = [units_of(np.ascontiguousarray(a))[0] for a in (kvi, q, u, v)]

    def mlp_blocks(layer):
        up = units_of(np.asarray(inputs["ff_w1"])[layer])[0].reshape(4, 8, P, KT, P)
        down = units_of(np.asarray(inputs["ff_w2"])[layer])
        return np.stack([up, down], axis=1).reshape(64, P, KT, P)

    pw1 = units_of(np.asarray(inputs["od_w_pw1"])[0])[0].reshape(2, 8, P, KT, P).transpose(1, 0, 2, 3, 4)
    weights = np.concatenate(z_blocks + [units_of(np.asarray(inputs["ev_w_out"])[0])[0], mlp_blocks(0),
                                         pw1.reshape(16, P, KT, P), units_of(np.asarray(inputs["od_w_pw2"])[0])[0],
                                         mlp_blocks(1)])
    gains = np.stack([np.asarray(a).reshape(KT, P).T for a in (
        inputs["ev_g_norm"][0], inputs["ff_g_norm"][0], inputs["od_g_norm"][0], inputs["od_g_conv"][0],
        inputs["ff_g_norm"][1], inputs["od_b_dw"][0])], axis=1)
    g_kidx = np.concatenate([np.asarray(inputs["ev_g_kidx"])[0], np.zeros(HD - ID, np.float32)])
    g_head = np.stack([np.asarray(inputs["ev_g_q"])[0], np.asarray(inputs["ev_g_k"])[0], g_kidx])
    arrays = {
        "x_t": x[0].T.reshape(KT, P, SEQ),
        "positions": np.asarray(inputs["positions"])[0].reshape(8, P).T,
        "inv_freq": np.broadcast_to((10000.0 ** (-np.arange(HD // 2) * 2.0 / HD)).astype(np.float32), (P, HD // 2)),
        "weights": weights,
        "gains": gains,
        "g_head": np.broadcast_to(g_head[None], (P, 3, HD)),
        "g_vb": np.broadcast_to(np.asarray(inputs["ev_g_vb"])[0][None], (P, HALF)),
        "w_s": np.asarray(inputs["ev_w_s"])[0].transpose(2, 0, 1),
        "b_s": np.asarray(inputs["ev_b_s"])[0].T,
        "w_dw": np.asarray(inputs["od_w_dw"])[0].reshape(CONV, KT, P).transpose(2, 1, 0),
    }
    arrays = {name: np.ascontiguousarray(a) for name, a in arrays.items()}
    nc = bacc.Bacc("TRN2", target_bir_lowering=False, num_devices=1)
    args = [nc.dram_tensor(name, a.shape, mybir.dt.from_np(a.dtype), kind="ExternalInput").ap()
            for name, a in arrays.items()]
    out_t = nc.dram_tensor("out_t", (KT, P, SEQ), F32, kind="ExternalOutput").ap()
    build(nc, *args, out_t)
    r = run_bass_kernel_spmd(nc, [arrays], core_ids=[0])
    return np.ascontiguousarray(r.results[0]["out_t"].reshape(D, SEQ).T)[None]
```

```python
from contextlib import ExitStack

import numpy as np

import concourse.bass as bass
from concourse import mybir

ALU = mybir.AluOpType
ACT = mybir.ActivationFunctionType
F32 = mybir.dt.float32
F32R = mybir.dt.float32r
I32 = mybir.dt.int32
AX_X = mybir.AxisListType.X

P = 128
SEQ = 1024
D = 1024
KT = D // P
HALF = 512
HT = HALF // P
HEADS, HD = 8, 64
IH, ID = 8, 32
TOPK = 256
ROUNDS = TOPK // 8
GROUPS, GD = 8, 64
IDX_SCALE = (IH ** -0.5) * (ID ** -0.5)
CONV = 31
EPS = 1e-6
K0, V0, QI0, KI0, WI0 = 0, 64, 128, 384, 416
C0 = 424
CHUNK_COLS = [C0, 512, 512, 512]
KV, QC, UC, VC = range(4)
NSTEP = 32
NEG = -1e30
TAKEN = -3e38
G_EV, G_FF0, G_OD, G_CONV, G_FF1, B_DW = range(6)

ZB = 16
WOUT, FF0, PW1, PW2, FF1 = ZB, ZB + 8, ZB + 72, ZB + 88, ZB + 96
NBLOCK = ZB + 160
STAGES = [("wout", 0, WOUT, 8), ("ff0", 0, FF0, 64), ("wout", 1, WOUT, 8), ("pw1", 0, PW1, 16),
          ("ff0", 1, FF0, 64), ("pw1", 1, PW1, 16),
          ("pw2", 0, PW2, 8), ("ff1", 0, FF1, 64), ("pw2", 1, PW2, 8), ("ff1", 1, FF1, 64)]
FIRST = {}
_n = 0
for _name, _half, _block, _count in STAGES:
    FIRST[_name, _half] = _n
    _n += _count
NUNIT = _n
AHEAD = 3


CAT_AT, Q_AT = 4, 6


def transposition_groups():
    groups = []
    for t in range(8):
        groups.append(("k", t, 0))
        if t >= 2:
            groups += [("qi", t, 0), ("qi", t, 1)]
    for half in range(2):
        groups += [("q", 4 * half, 0), ("q", 4 * half, 1)]
        for a in range(32 * half, 32 * half + 34):
            t, h = a // 8, a % 8
            if a < 32 * half + 32:
                if h == CAT_AT and t % 4:
                    groups += [("cat", t - 1, 0), ("cat", t - 1, 1)]
                if h == Q_AT and t % 4 < 3:
                    groups += [("q", t + 1, 0), ("q", t + 1, 1)]
            if a >= 32 * half + 2:
                groups += [("p", a - 2, g) for g in range(((a - 2) // 8 + 4) // 4)]
        groups += [("cat", 4 * half + 3, 0), ("cat", 4 * half + 3, 1)]
    return {key: n for n, key in enumerate(groups)}


TR = transposition_groups()
CATS = [n for key, n in TR.items() if key[0] == "cat"]
LOGITS = [0, 0, 0]
for _t in range(2, 8):
    LOGITS.append(LOGITS[-1] + IH * ((_t + 4) // 4))
UPS = {("ff0", 0): 0, ("ff0", 1): 32, ("ff1", 0): 64, ("ff1", 1): 96}
CONV_IN = {("ff0", 1): "conv0", ("ff1", 0): "conv1"}
CONSTS = 3
CONSTS_IN = 16 * 7
CREDIT = 2


def wait_apart(engine, sem, value, passed):
    engine.wait_ge(sem, value)
    engine.sem_inc(passed, 1)


def flat(buf, part, k):
    return buf[:, k, :] if part is None else buf[:, part, k, :]


def build(nc, x_t, positions, inv_freq, weights, gains, g_head, g_vb, w_s, b_s, w_dw, out_t):
    with ExitStack() as ctx:
        base = (nc.sbuf_base + 31) // 32 * 32

        def put(name, at, shape, dt=F32):
            size = int(np.prod(shape[1:])) * 4
            return nc.alloc_sbuf_tensor_at(name, shape, dt, offset=base + at), at + size

        KB = 1024
        h_buf, _ = put("h_buf", 0, [P, 2, KT, HALF], F32R)
        hid_buf, _ = put("hid_buf", 32 * KB, [P, 2, KT, HALF], F32R)
        w_buf, _ = put("w_buf", 64 * KB, [P, 2, KT, HALF], F32R)
        raw, _ = put("raw", 96 * KB, [P, 2, KT, P])
        xt0, _ = put("xt0", 104 * KB, [P, KT, HALF])
        xt1, _ = put("xt1", 120 * KB, [P, KT, HALF])
        xt = [xt0, xt1]
        zt, a = put("zt", 104 * KB, [P, 2, C0])
        qz, a = put("qz", a, [P, HALF])
        tmp, a = put("tmp", a, [P, 2, HALF])
        pool_tmp, a = put("pool_tmp", a, [P, HALF])
        junk, a = put("junk", a, [P, HD + ID])
        k_stack, a = put("k_stack", a, [P, 3, HD], F32R)
        ki_stack, a = put("ki_stack", a, [P, 3, ID], F32R)
        qi_stack, a = put("qi_stack", a, [P, IH, 3, ID], F32R)
        assert a <= 120 * KB
        q_tok, _ = put("q_tok", 120 * KB, [P, 8, HEADS, HD])
        x_in, _ = put("x_in", 120 * KB, [P, KT, HALF])
        s_buf, a = put("s_buf", 0, [P, 2, SEQ])
        p_buf, a = put("p_buf", a, [P, 2, SEQ])
        pt_buf, a = put("pt_buf", a, [P, 2, SEQ])
        q_t0, a = put("q_t0", a, [P, HEADS, P], F32R)
        q_stack, a = put("q_stack", a, [P, HEADS, 2, HD], F32R)
        assert a <= 32 * KB
        k_t, a = put("k_t", 136 * KB, [P, SEQ], F32R)
        k_lo_t, a = put("k_lo_t", a, [HD, SEQ], F32R)
        v_tok, a = put("v_tok", a, [P, 8, HD])
        score = [None, None]
        for t in range(2, 8):
            s, a = put(f"score{t}", a, [P, P * (t + 1)])
            score.append(s)
        b_tok, a = put("b_tok", a, [P, 8, HALF])
        y_buf, c = put("y_buf", 136 * KB, [P, KT, CONV - 1 + HALF])
        c_buf, c = put("c_buf", c, [P, KT, HALF])
        u_ring, c = put("u_ring", c, [P, 2, HALF])
        v_ring, c = put("v_ring", c, [P, 2, HALF])
        assert c <= a
        ident, a = put("ident", a, [P, P])
        ones, a = put("ones", a, [P, P])
        tri, a = put("tri", a, [P, P])
        gain, a = put("gain", a, [P, 6, KT])
        wdw, a = put("wdw", a, [P, KT, CONV])
        small, a = put("small", a, [P, 192])
        sq_sum, a = put("sq_sum", a, [P, HALF])
        sq_ring, a = put("sq_ring", a, [P, 2, HALF])
        again = a
        qi_t, a = put("qi_t", again, [P, IH, P], F32R)
        ki_t, a = put("ki_t", a, [P, SEQ], F32R)
        ws, a = put("ws", a, [P, GROUPS, P])
        cos, a = put("cos", a, [P, 8, HD // 2])
        sin, a = put("sin", a, [P, 8, HD // 2])
        gvb, a = put("gvb", a, [P, HALF])
        gh, a = put("gh", a, [P, 3, HD])
        bs, a = put("bs", a, [P, GROUPS])
        pos_i, a = put("pos_i", a, [P, 8], I32)
        inv_f, a = put("inv_f", a, [P, HD // 2])
        end_z = a
        rms_bc, a = put("rms_bc", again, [P, HALF])
        conv_bc, a = put("conv_bc", a, [P, HALF])
        at_t_ring = a
        t_ring, a = put("t_ring", a, [P, 2, HALF])
        s_ring, a = put("s_ring", a, [P, 2, HALF])
        a_tok, a = put("a_tok", a, [P, HALF])
        c_sum, a = put("c_sum", a, [P, HALF])
        diag_buf, a = put("diag_buf", a, [P, HALF])
        q_t1 = nc.alloc_sbuf_tensor_at("q_t1", [P, HEADS, P], F32R, offset=base + at_t_ring)
        q_t = [q_t0, q_t1]
        assert max(a, end_z) + base <= nc.sbuf_usable_end, (a, end_z)

        diag = diag_buf[:]

        def yflat(k, at):
            return y_buf[:, k, bass.ds(at, HALF)]

        def gflat(g, k):
            return gain[:, g, bass.ds(k, 1)]

        psum = nc.alloc_psum_tensor("psum", [P, 8, HALF], F32)

        pos_f = small[:, 0:8]
        r_tok = small[:, 8:16]
        st_v, st_y, st_a = small[:, 16:24], small[:, 24:32], small[:, 32:40]
        top8 = [small[:, 48:56], small[:, 40:48]]
        row_sum = [small[:, 56:64], small[:, 108:116]]
        neg_max = small[:, 64:66]
        row_max = small[:, 66:68]
        r_inv = small[:, 72:80]
        vsum = small[:, 80:81]
        r_q = small[:, 116:180].rearrange("p (t h) -> p t h", t=8)
        st_k = small[:, 180:184].rearrange("p (a b) -> p a b", a=2)
        w_idx = [small[:, 84 + 8 * n:92 + 8 * n] for n in range(3)]

        def sem(name):
            return ctx.enter_context(nc.semaphore(name))

        consts_in = sem("consts_in")
        consts_up = sem("consts_up")
        rope_up = sem("rope_up")
        rope_arg = sem("rope_arg")
        x_in_full = [sem(f"x_in_full{n}") for n in range(KT)]
        gains_in = sem("gains_in")
        ws_up = sem("ws_up")
        qi_done = sem("qi_done")
        q_done = sem("q_done")
        landed = [sem("landed0"), sem("landed1")]
        hi_up = sem("hi_up")
        lo_up = sem("lo_up")
        prep_hi = sem("prep_hi")
        prep_sq = sem("prep_sq")
        prep_lo = sem("prep_lo")
        prep_sum = sem("prep_sum")
        sum_clear = sem("sum_clear")
        stat_up = sem("stat_up")
        stat_diag = sem("stat_diag")
        stat_bc = sem("stat_bc")
        z_up = sem("z_up")
        z_read = sem("z_read")
        z_proc = sem("z_proc")
        z_sq = sem("z_sq")
        z_vsq = sem("z_vsq")
        tr_up = sem("tr_up")
        tr_read = sem("tr_read")
        logit_up = sem("logit_up")
        logit_relu = sem("logit_relu")
        logit_used = sem("logit_used")
        spat_up = sem("spat_up")
        spat_used = sem("spat_used")
        q_split = sem("q_split")
        qk_up = sem("qk_up")
        qk_masked = sem("qk_masked")
        neg_up = sem("neg_up")
        exp_up = sem("exp_up")
        pv_up = sem("pv_up")
        att_norm = sem("att_norm")
        cat_hi = sem("cat_hi")
        cat_lo = sem("cat_lo")
        unit_up = sem("unit_up")
        unit_read = sem("unit_read")
        squared = sem("squared")
        hid_hi = sem("hid_hi")
        hid_lo = sem("hid_lo")
        gate_up = sem("gate_up")
        y_up = sem("y_up")
        topk_step = sem("topk_step")
        conv_step = sem("conv_step")
        conv_sq = sem("conv_sq")
        conv_sum = sem("conv_sum")
        act_in = sem("act_in")
        act_silu = sem("act_silu")
        act_hi = sem("act_hi")
        act_lo = sem("act_lo")
        x_full = sem("x_full")
        out_sem = sem("out_sem")
        passed_v = sem("passed_v")
        passed_s = sem("passed_s")
        dve_chain = sem("dve_chain")
        act_chain = sem("act_chain")
        pool_chain = sem("pool_chain")

        block = ctx.enter_context(nc.Block())

        PREPS = ["z0", "z1", "ff0_0", "pw1_0", "ff0_1", "pw1_1", "ff1_0", "ff1_1"]
        PREP = {name: n for n, name in enumerate(PREPS)}
        STATS = ["z0", "z1", "ff0_0", "pw1_0", "ff0_1", "pw1_1", "conv0", "ff1_0", "conv1", "ff1_1"]
        STAT = {name: n for n, name in enumerate(STATS)}
        BCS = [s for s in STATS if s[0] != "z"]
        BC = {name: n for n, name in enumerate(BCS)}
        OPERAND = {("ff0", 0): (h_buf, hid_buf), ("pw1", 0): (h_buf, None), ("ff0", 1): (hid_buf, h_buf),
                   ("pw1", 1): (hid_buf, None), ("pw2", 0): (h_buf, hid_buf), ("ff1", 0): (hid_buf, h_buf),
                   ("pw2", 1): (hid_buf, h_buf), ("ff1", 1): (h_buf, hid_buf)}

        def name_of(stage, half):
            return f"{stage}_{half}"

        @block.sync
        def _(sp):
            def unit(w, block_index, slot):
                if not isinstance(w, int) or w >= 2:
                    sp.wait_ge(lo_up, w - 1)
                sp.dma_start(raw[:, slot], weights[block_index]).then_inc(landed[slot], 16)

            def x_tile(half, k):
                slot = k if half == 0 else 4 + k % 4
                n = half * KT + k
                if half:
                    sp.wait_ge(prep_lo, KT if k < 4 else n - 3)
                    sp.wait_ge(prep_sq, KT if k < 4 else n - 3)
                sp.dma_start(x_in[:, slot], x_t[k, :, half * HALF:(half + 1) * HALF]).then_inc(x_in_full[slot], 16)

            sp.dma_start(gain[:], gains).then_inc(gains_in, 16)
            for w in range(4):
                x_tile(0, 2 * w)
                x_tile(0, 2 * w + 1)
                unit(w, w, w % 2)
            for dst, src in ((inv_f[:], inv_freq), (pos_i[:], positions), (gh[:], g_head), (gvb[:], g_vb),
                             (ws[:], w_s), (bs[:], b_s), (wdw[:], w_dw)):
                sp.dma_start(dst, src).then_inc(consts_in, 16)
            with sp.Fori(2, 8) as i:
                for r in range(2):
                    unit(2 * i + r, 2 * i + r, r)
            with sp.Fori(0, 2) as i:
                for r in range(2):
                    unit(16 + 2 * i + r, 2 * i + r, r)
            for k in range(KT):
                x_tile(1, k)
            with sp.Fori(2, 8) as i:
                for r in range(2):
                    unit(16 + 2 * i + r, 2 * i + r, r)

            def stream(first, first_block, start, count):
                with sp.Fori(start // 2, count // 2) as i:
                    for r in range(2):
                        unit(32 + first + 2 * i + r, first_block + 2 * i + r, r)

            for name, half, first_block, count in STAGES:
                first = FIRST[name, half]
                if (name, half) == ("wout", 0):
                    stream(first, first_block, 0, 4)
                    sp.wait_ge(z_read, NSTEP)
                    sp.wait_ge(spat_used, 8)
                    sp.wait_ge(logit_used, LOGITS[8])
                    sp.wait_ge(tr_read, TR["q", 0, 0])
                    sp.dma_start(xt0[:], x_t[:, :, 0:HALF].rearrange("k p n -> p k n")).then_inc(x_full, 16)
                    stream(first, first_block, 4, count)
                    continue
                if (name, half) == ("wout", 1):
                    stream(first, first_block, 0, 4)
                    sp.wait_ge(q_split, 8)
                    sp.dma_start(xt1[:], x_t[:, :, HALF:SEQ].rearrange("k p n -> p k n")).then_inc(x_full, 16)
                    stream(first, first_block, 4, count)
                    continue
                stream(first, first_block, 0, count)
                if (name, half) == ("pw2", 1):
                    sp.wait_ge(unit_read, FIRST["ff1", 0] + 64)
                    sp.dma_start(out_t[:, :, 0:HALF].rearrange("k p n -> p k n"), xt0[:]).then_inc(out_sem, 16)
            for k in range(KT):
                sp.wait_ge(unit_read, NUNIT - KT + 1 + k)
                sp.dma_start(out_t[k, :, HALF:SEQ], xt1[:, k]).then_inc(out_sem, 16)
            sp.wait_ge(out_sem, 16 * (1 + KT))

        @block.tensor
        def _(pe):
            def products(acc, lhs_hi, lhs_lo, rhs_hi, rhs_lo, first, last):
                nc.tensor.matmul(acc, lhs_hi, rhs_hi, start=first, stop=False)
                nc.tensor.matmul(acc, lhs_hi, rhs_lo, start=False, stop=False)
                return nc.tensor.matmul(acc, lhs_lo, rhs_hi, start=False, stop=last)

            def sums_by_token(name, sums):
                n = STAT[name]
                for j in range(HT):
                    mm = nc.tensor.matmul(psum[:, 7, j:j + 1], sums[:, j * P:(j + 1) * P], ones[:, 0:1],
                                          start=True, stop=True)
                mm.then_inc(stat_up, 1)

            def broadcast_rms():
                mm = nc.tensor.matmul(psum[:, 7, :], ones[:], diag, start=True, stop=True)
                mm.then_inc(stat_bc, 1)

            def transpose_group(key, parts):
                n = TR[key]
                if n >= 3:
                    pe.wait_ge(tr_read, n - 2)
                    if key[0] in ("p", "q", "cat"):
                        done = [at for at in CATS if at <= n - 3]
                        if done:
                            pe.wait_ge(cat_lo, len(done))
                for dst, src in parts(psum[:, 4 + n % 3, :]):
                    tr = nc.tensor.transpose(dst, src, ident[:])
                tr.then_inc(tr_up, 1)

            pe.wait_ge(consts_up, CONSTS)

            def project(s):
                half, c, j = s // 16, s // 4 % 4, s % 4
                wb = (hid_buf, w_buf)[c % 2]
                n = CHUNK_COLS[c]
                if s >= 2:
                    pe.wait_ge(z_read, s - 1)
                if j == 0:
                    pe.wait_ge(lo_up, 4 * (s // 4 + 1))
                acc = psum[:, s % 2, 0:n]
                for k in range(KT):
                    if c == KV and j == 0:
                        pe.wait_ge(prep_lo, half * KT + k + 1)
                    mm = products(acc, h_buf[:, 0, k, j * P:(j + 1) * P], h_buf[:, 1, k, j * P:(j + 1) * P],
                                  wb[:, 0, k, 0:n], wb[:, 1, k, 0:n], k == 0, k == KT - 1)
                mm.then_inc(z_up, 1)

            def turn_keys(t):
                pe.wait_ge(z_proc, 16 * (t // 4) + t % 4 + 1)
                transpose_group(("k", t, 0), lambda bank: [
                    (bank[:, 0:P], k_stack[:, 0:2, :].bitcast(F32).rearrange("p a d -> p (a d)")),
                    (bank[0:HD, P:2 * P], k_stack[:, 2, :].bitcast(F32)),
                    (bank[0:3 * ID, 2 * P:3 * P], ki_stack[:].bitcast(F32).rearrange("p a d -> p (a d)"))])
                if t >= 2:
                    pe.wait_ge(qi_done, t - 1)
                    for g in range(2):
                        transpose_group(("qi", t, g), lambda bank: [
                            (bank[0:3 * ID, i * P:(i + 1) * P],
                             qi_stack[:, 4 * g + i].bitcast(F32).rearrange("p a d -> p (a d)")) for i in range(4)])

            def index_logits(t):
                n = LOGITS[t]
                pe.wait_ge(tr_read, TR["qi", t, 1] + 1)
                for h in range(IH):
                    for c0 in range(0, P * (t + 1), HALF):
                        c1 = min(c0 + HALF, P * (t + 1))
                        if n >= 2:
                            pe.wait_ge(logit_relu, n - 1)
                        nc.tensor.matmul(psum[:, 2 + n % 2, 0:c1 - c0], qi_t[0:3 * ID, h, :], ki_t[0:3 * ID, c0:c1],
                                         start=True, stop=True).then_inc(logit_up, 1)
                        n += 1

            def spatial(t):
                pe.wait_ge(z_proc, 16 * (t // 4) + 12 + t % 4 + 1)
                if t == 0:
                    pe.wait_ge(ws_up, 1)
                if t >= 1:
                    pe.wait_ge(spat_used, t)
                for g in range(GROUPS):
                    mm = nc.tensor.matmul(psum[:, 7, g * GD:(g + 1) * GD], ws[:, g, :], qz[:, g * GD:(g + 1) * GD],
                                          start=True, stop=True)
                mm.then_inc(spat_up, 1)

            for s in range(NSTEP + 2):
                if s < NSTEP:
                    project(s)
                for back, job in ((1, turn_keys), (2, index_logits)):
                    b = s - back
                    if 0 <= b < NSTEP and b // 4 % 4 == KV:
                        t = b // 16 * 4 + b % 4
                        if job is turn_keys or t >= 2:
                            job(t)
                b = s - 1
                if 0 <= b < NSTEP and b // 4 % 4 == VC:
                    spatial(b // 16 * 4 + b % 4)
                if s in (0, 16):
                    pe.wait_ge(prep_sum, KT * (s // 16 + 1))
                    if s:
                        pe.wait_ge(spat_used, 4)
                    sums_by_token(f"z{s // 16}", sq_sum)

            def attention(half):
                pe.wait_ge(spat_used, 8)
                if half:
                    pe.wait_ge(unit_read, FIRST["wout", 1])

                def cat(t):
                    pe.wait_ge(att_norm, t + 1)
                    for g, src in ((0, a_tok[:]), (1, b_tok[:, t, :])):
                        transpose_group(("cat", t, g), lambda bank: [
                            (bank[:, i * P:(i + 1) * P], src[:, i * P:(i + 1) * P]) for i in range(4)])

                def queries(t):
                    pe.wait_ge(q_split, t + 1)
                    for g in range(2):
                        transpose_group(("q", t, g), lambda bank: [
                            (bank[:, i * P:(i + 1) * P],
                             q_stack[:, 4 * g + i].bitcast(F32).rearrange("p a d -> p (a d)")) for i in range(4)])

                def scores(a):
                    t, h = a // 8, a % 8
                    if h == 0:
                        pe.wait_ge(tr_read, TR["q", t, 1] + 1)
                    if a >= 2:
                        pe.wait_ge(qk_masked, a - 1)
                    for c0 in range(0, P * (t + 1), HALF):
                        c1 = min(c0 + HALF, P * (t + 1))
                        dst = psum[:, 2 * (a % 2) + c0 // HALF, 0:c1 - c0]
                        nc.tensor.matmul(dst, q_t[t % 2][:, h, :], k_t[:, c0:c1], start=True, stop=False)
                        mm = nc.tensor.matmul(dst, q_t[t % 2][0:HD, h, :], k_lo_t[:, c0:c1], start=False, stop=True)
                    mm.then_inc(qk_up, 1)

                def turn_probs(a):
                    t = a // 8
                    pe.wait_ge(exp_up, a + 1)
                    for g in range((t + 4) // 4):
                        transpose_group(("p", a, g), lambda bank: [
                            (bank[:, (b % 4) * P:(b % 4 + 1) * P], p_buf[:, a % 2, b * P:(b + 1) * P])
                            for b in range(4 * g, min(4 * g + 4, t + 1))])

                def values(a):
                    t, h = a // 8, a % 8
                    pe.wait_ge(tr_read, TR["p", a, (t + 4) // 4 - 1] + 1)
                    if h == 0 and t % 4:
                        pe.wait_ge(att_norm, t)
                    for b in range(t + 1):
                        mm = nc.tensor.matmul(psum[:, 7, h * HD:(h + 1) * HD], pt_buf[:, a % 2, b * P:(b + 1) * P],
                                              v_tok[:, b, :], start=(b == 0), stop=(b == t))
                    mm.then_inc(pv_up, 1)

                first, end = 32 * half, 32 * half + 32
                queries(4 * half)
                for a in range(first, end + 3):
                    if a < end:
                        if a % 8 == CAT_AT and a // 8 % 4:
                            cat(a // 8 - 1)
                        if a % 8 == Q_AT and a // 8 % 4 < 3:
                            queries(a // 8 + 1)
                        scores(a)
                    if first + 2 <= a < end + 2:
                        turn_probs(a - 2)
                    if a >= first + 3:
                        values(a - 3)
                cat(4 * half + 3)

            def unit(m, slot, operand, ready=None, ready_at=0):
                pe.wait_ge(lo_up, 32 + m + 1)
                if not isinstance(m, int) or m >= 4:
                    pe.wait_ge(unit_read, m - 3)
                for k in range(KT):
                    if ready is not None:
                        pe.wait_ge(ready, ready_at + k + 1)
                    cols = slice(slot * P, (slot + 1) * P)
                    mm = products(psum[:, slot, :], w_buf[:, 0, k, cols], w_buf[:, 1, k, cols],
                                  operand[:, 0, k, :], operand[:, 1, k, :], k == 0, k == KT - 1)
                mm.then_inc(unit_up, 1)

            def units(first, count, operand, ready=None, ready_at=0, after=()):
                for r in range(4):
                    unit(first + r, r, operand, ready if r == 0 else None, ready_at)
                    for at, job in after:
                        if at == r:
                            job()
                if count > 4:
                    with pe.Fori(1, count // 4) as i:
                        for r in range(4):
                            unit(first + 4 * i + r, r, operand)

            def rms_jobs(name, prep):
                def take():
                    pe.wait_ge(prep_sum, KT * (PREP[prep] + 1))
                    sums_by_token(name, sq_sum)

                def spread():
                    pe.wait_ge(stat_diag, STAT[name] + 1)
                    broadcast_rms()
                return ((0, take), (2, spread))

            def conv_rms_jobs(half):
                def take():
                    pe.wait_ge(conv_sum, CREDIT + 8 * (half + 1))
                    sums_by_token(f"conv{half}", c_sum)

                def spread():
                    pe.wait_ge(stat_diag, STAT[f"conv{half}"] + 1)
                    broadcast_rms()
                return ((0, take), (1, spread))

            def mlp(stage, half, operand, hidden):
                first = FIRST[stage, half]
                name = name_of(stage, half)
                ups = UPS[stage, half]
                for q in range(4):
                    if q == 0:
                        units(first, 8, operand, prep_lo, KT * PREP[name], rms_jobs(name, name))
                    else:
                        units(first + 16 * q, 8, operand)
                    late = q == 3 and (stage, half) == ("ff1", 0)
                    units(first + 16 * q + 8, 8, hidden, hid_lo, CREDIT + ups + 8 * q,
                          conv_rms_jobs(1) if late else ())

            for name, half, _, count in STAGES:
                first = FIRST[name, half]
                if (name, half) == ("wout", 0):
                    attention(0)
                if (name, half) == ("wout", 1):
                    attention(1)
                if name == "wout":
                    pe.wait_ge(cat_lo, 8 * (half + 1))
                    units(first, 8, hid_buf)
                elif name in ("ff0", "ff1"):
                    mlp(name, half, *OPERAND[name, half])
                elif name == "pw1":
                    n = name_of(name, half)
                    operand = OPERAND[name, half][0]
                    units(first, 8, operand, prep_lo, KT * PREP[n], rms_jobs(n, n))
                    units(first + 8, 8, operand, after=conv_rms_jobs(0) if half else ())
                else:
                    units(first, 8, OPERAND[name, half][0], act_lo, CREDIT + 8 * half)

        @block.gpsimd
        def _(pool):
            pool.sem_inc(hid_lo, CREDIT)
            pool.sem_inc(y_up, CREDIT)
            pool.sem_inc(act_lo, CREDIT)
            nc.gpsimd.memset(ident[:], 0.0).then_inc(pool_chain, 1)
            nc.gpsimd.memset(tri[:], 0.0).then_inc(pool_chain, 1)
            nc.gpsimd.memset(ones[:], 1.0).then_inc(consts_up, 1)
            pool.wait_ge(pool_chain, 2)
            nc.gpsimd.affine_select(out=ident[:], in_=ident[:], compare_op=ALU.not_equal, fill=1.0, base=0,
                                    pattern=[[-1, P]], channel_multiplier=1).then_inc(consts_up, 1)
            nc.gpsimd.affine_select(out=tri[:], in_=tri[:], compare_op=ALU.is_ge, fill=NEG, base=0,
                                    pattern=[[-1, P]], channel_multiplier=1).then_inc(consts_up, 1)
            def split_lo(w, raw_slot, dst_hi, dst_lo):
                pool.wait_ge(hi_up, w + 1)
                nc.gpsimd.tensor_tensor(dst_lo, raw[:, raw_slot], dst_hi.bitcast(F32), ALU.subtract
                                        ).then_inc(lo_up, 1)

            chain = [2]

            def link(ins):
                chain[0] += 1
                ins.then_inc(pool_chain, 1)
                pool.wait_ge(pool_chain, chain[0])

            def split_z(w):
                wb, cols = (hid_buf, w_buf)[w // 4 % 2], slice(w % 4 * P, (w % 4 + 1) * P)
                split_lo(w, w % 2, wb[:, 0, :, cols], wb[:, 1, :, cols])

            T = nc.gpsimd.tensor_tensor

            def rope(x, t, heads, d):
                h = d // 2
                c = cos[:, t, ::HD // d][:, None, :].broadcast_to([P, heads, h])
                s = sin[:, t, ::HD // d][:, None, :].broadcast_to([P, heads, h])
                other = pool_tmp[:, 0:heads * d].rearrange("p (n d) -> p n d", d=d)
                T(other[:, :, 0:h], x[:, :, h:d], s, ALU.mult)
                link(T(other[:, :, h:d], x[:, :, 0:h], s, ALU.mult))
                T(x[:, :, 0:h], x[:, :, 0:h], c, ALU.mult)
                link(T(x[:, :, h:d], x[:, :, h:d], c, ALU.mult))
                T(x[:, :, 0:h], x[:, :, 0:h], other[:, :, 0:h], ALU.subtract)
                link(T(x[:, :, h:d], x[:, :, h:d], other[:, :, h:d], ALU.add))

            def index_queries(s, t):
                pool.wait_ge(z_read, s + 1)
                pool.wait_ge(rope_up, 2)
                if t > 2:
                    pool.wait_ge(tr_up, TR["qi", t - 1, 1] + 1)
                q = zt[:, t % 2, QI0:KI0].rearrange("p (n d) -> p n d", n=IH)
                rope(q, t, IH, ID)
                nc.gpsimd.tensor_copy(qi_stack[:, :, 2, :], q)
                link(nc.gpsimd.tensor_copy(qi_stack[:, :, 0, :], q))
                T(qi_stack[:, :, 1, :], q, qi_stack[:, :, 0, :].bitcast(F32), ALU.subtract).then_inc(qi_done, 1)

            def queries(s, t):
                pool.wait_ge(z_read, s + 1)
                pool.wait_ge(z_sq, t + 1)
                link(T(q_tok[:, t], q_tok[:, t], gh[:, 0, :][:, None, :].broadcast_to([P, HEADS, HD]), ALU.mult))
                rope(q_tok[:, t], t, HEADS, HD)
                pool.sem_inc(q_done, 1)

            for w in range(4):
                split_z(w)
            pool.wait_ge(consts_in, CONSTS_IN)
            nc.gpsimd.affine_select(out=ws[:], in_=ws[:], compare_op=ALU.is_ge, fill=0.0, base=0,
                                    pattern=[[0, GROUPS], [1, P]], channel_multiplier=-1).then_inc(ws_up, 1)
            for s in range(NSTEP):
                if s < 28:
                    split_z(s + 4)
                c, t = s // 4 % 4, s // 16 * 4 + s % 4
                if c == KV and t >= 2:
                    index_queries(s, t)
                if s % 16 in (5, 7, 9, 11):
                    j = (s % 16 - 5) // 2
                    queries(s // 16 * 16 + 4 + j, s // 16 * 4 + j)

            def split_main(m, slot):
                cols = slice(slot * P, (slot + 1) * P)
                split_lo(32 + m, slot % 2, w_buf[:, 0, :, cols], w_buf[:, 1, :, cols])

            for m in range(AHEAD):
                split_main(m, m)

            def units(first, count, job=None, last=False):
                def group(i):
                    for r in range(4):
                        if not (last and isinstance(i, int) and i == count // 4 - 1 and r >= 4 - AHEAD):
                            split_main(first + 4 * i + r + AHEAD, (r + AHEAD) % 4)
                        if job:
                            job(i, r)
                with pool.Fori(0, count // 4 - last) as i:
                    group(i)
                if last:
                    group(count // 4 - 1)

            def mlp(stage, half, hidden):
                first, ups = FIRST[stage, half], UPS[stage, half]
                for q in range(4):
                    def hidden_lo(i, r):
                        n = ups + 8 * q + 4 * i + r
                        pool.wait_ge(hid_hi, n + 1)
                        k = 4 * i + r
                        nc.gpsimd.tensor_tensor(flat(hidden, 1, k), s_ring[:, r % 2],
                                                flat(hidden, 0, k).bitcast(F32), ALU.subtract).then_inc(hid_lo, 1)

                    units(first + 16 * q, 8, hidden_lo)
                    job = None
                    if q == 3 and (stage, half) == ("ff1", 0):
                        job = swish_lo(1, hid_buf)
                    units(first + 16 * q + 8, 8, job, last=(q == 3 and (stage, half) == ("ff1", 1)))

            def swish_lo(half, dst):
                def job(i, r):
                    n = 8 * half + 4 * i + r
                    k = 4 * i + r
                    pool.wait_ge(act_hi, n + 1)
                    nc.gpsimd.tensor_tensor(flat(dst, 1, k), v_ring[:, r % 2], flat(dst, 0, k).bitcast(F32),
                                            ALU.subtract).then_inc(act_lo, 1)
                return job

            for name, half, _, count in STAGES:
                first = FIRST[name, half]
                if name in ("ff0", "ff1"):
                    mlp(name, half, OPERAND[name, half][1])
                elif name == "pw1":
                    if half == 0:
                        pool.wait_ge(cat_lo, 16)
                        pool.wait_ge(pv_up, 64)
                        nc.gpsimd.memset(y_buf[:, :, 0:CONV - 1], 0.0).then_inc(y_up, 1)
                    else:
                        pool.wait_ge(conv_step, CONV * KT)
                        nc.gpsimd.tensor_copy(y_buf[:, :, 0:CONV - 1], y_buf[:, :, HALF:HALF + CONV - 1]
                                              ).then_inc(y_up, 1)

                    def gated(part):
                        def job(i, r):
                            if r % 2:
                                k = 4 * part + 2 * i + r // 2
                                n = 8 * half + k
                                pool.wait_ge(gate_up, n + 1)
                                if half:
                                    pool.wait_ge(y_up, CREDIT + 10)
                                nc.gpsimd.tensor_tensor(yflat(k, CONV - 1), t_ring[:, r // 2], s_ring[:, r // 2],
                                                        ALU.mult).then_inc(y_up, 1)
                        return job

                    units(first, 8, gated(0))
                    swish = swish_lo(0, h_buf) if half else None
                    gate = gated(1)

                    def both(i, r):
                        gate(i, r)
                        if swish:
                            swish(i, r)
                    units(first + 8, 8, both)
                else:
                    units(first, 8)

        @block.scalar
        def _(act):
            chain = [0]

            def link(ins):
                chain[0] += 1
                ins.then_inc(act_chain, 1)
                act.wait_ge(act_chain, chain[0])

            act.sem_inc(squared, CREDIT)
            act.sem_inc(act_silu, CREDIT)

            def prep(n0, k, src, dst, g, ready=None, ready_at=None):
                if ready is not None:
                    act.wait_ge(ready, ready_at)
                nc.scalar.activation(flat(dst, 0, k), src, ACT.Copy, scale=gflat(g, k)).then_inc(prep_hi, 1)

            def square(n0, k, ring, src):
                n = n0 + k
                if not isinstance(n, int) or n >= 2:
                    wait_apart(act, prep_sum, n - 1, passed_s)
                nc.scalar.activation(sq_ring[:, ring], src, ACT.Square).then_inc(prep_sq, 1)

            def split_hi(w, raw_slot, landings, dst):
                act.wait_ge(landed[raw_slot], 16 * landings)
                nc.scalar.activation(dst, raw[:, raw_slot], ACT.Copy).then_inc(hi_up, 1)

            def split_z(w):
                wb, cols = (hid_buf, w_buf)[w // 4 % 2], slice(w % 4 * P, (w % 4 + 1) * P)
                if w >= 8 and w % 4 == 0:
                    act.wait_ge(z_up, w - 4)
                split_hi(w, w % 2, w // 2 + 1, wb[:, 0, :, cols])

            def prep_x(half, k):
                if half and k == 0:
                    act.wait_ge(z_up, 16)
                    act.wait_ge(z_vsq, 4)
                slot = k if half == 0 else 4 + k % 4
                prep(KT * half, k, x_in[:, slot], h_buf, G_EV, x_in_full[slot],
                     16 * (1 + half * (1 if slot == k else 1) + half * (k >= 4)))
                square(KT * half, k, k % 2, x_in[:, slot])

            act.wait_ge(gains_in, 16)
            for w in range(4):
                prep_x(0, 2 * w)
                prep_x(0, 2 * w + 1)
                split_z(w)
            act.wait_ge(rope_arg, 2)
            for dst in (sin, cos):
                nc.scalar.activation(dst[:], dst[:], ACT.Sin).then_inc(rope_up, 1)

            def evacuate(s):
                half, c, j = s // 16, s // 4 % 4, s % 4
                t = 4 * half + j
                src, r = psum[:, s % 2, 0:CHUNK_COLS[c]], r_tok[:, t:t + 1]
                act.wait_ge(z_up, s + 1)
                if s % 16 == 0:
                    act.wait_ge(stat_diag, half + 1)
                if c == KV:
                    if t >= 2:
                        act.wait_ge(z_proc, s - 1)
                    if t >= 4:
                        act.wait_ge(qi_done, t - 3)
                    if s:
                        act.wait_ge(z_read, s)
                    for n, (at, d) in enumerate(((K0, HD), (KI0, ID))):
                        nc.scalar.activation(junk[:, n * HD:n * HD + d], src[:, at:at + d], ACT.Square, scale=r,
                                             accum_out=st_k[:, t % 2, n:n + 1])
                    nc.scalar.activation(v_tok[:, t, :], src[:, V0:V0 + HD], ACT.Copy, scale=r)
                    nc.scalar.activation(zt[:, t % 2], src, ACT.Copy, scale=r).then_inc(z_read, 1)
                elif c == QC:
                    act.wait_ge(z_proc, s)
                    if t == 4:
                        act.wait_ge(spat_up, 4)
                    nc.scalar.activation(qz[:], src, ACT.Square, scale=r).then_inc(z_sq, 1)
                    nc.scalar.activation(q_tok[:, t].rearrange("p h d -> p (h d)"), src, ACT.Copy, scale=r
                                         ).then_inc(z_read, 1)
                elif c == UC:
                    nc.scalar.activation(b_tok[:, t, :], src, ACT.Gelu_apprx_tanh, scale=r).then_inc(z_read, 1)
                else:
                    if t:
                        act.wait_ge(spat_up, t)
                    act.wait_ge(z_proc, s)
                    nc.scalar.activation(qz[:], src, ACT.Gelu_apprx_tanh, scale=r).then_inc(z_read, 1)
                    act.wait_ge(z_read, s + 1)
                    nc.scalar.activation(sq_ring[:, 0], qz[:], ACT.Square, accum_out=vsum).then_inc(z_vsq, 1)

            def keys_out(t):
                act.wait_ge(tr_up, TR["k", t, 0] + 1)
                bank, cols = psum[:, 4 + TR["k", t, 0] % 3, :], slice(t * P, (t + 1) * P)
                nc.scalar.copy(k_t[:, cols], bank[:, 0:P])
                nc.scalar.copy(k_lo_t[:, cols], bank[0:HD, P:2 * P])
                nc.scalar.copy(ki_t[0:3 * ID, cols], bank[0:3 * ID, 2 * P:3 * P]).then_inc(tr_read, 1)
                if t >= 2:
                    for g in range(2):
                        n = TR["qi", t, g]
                        act.wait_ge(tr_up, n + 1)
                        if t > 2:
                            act.wait_ge(logit_up, LOGITS[t])
                        nc.scalar.copy(qi_t[0:3 * ID, 4 * g:4 * g + 4, :].rearrange("p h n -> p (h n)"),
                                       psum[0:3 * ID, 4 + n % 3, :]).then_inc(tr_read, 1)

            def relus(t, s):
                act.wait_ge(z_proc, s)
                n = LOGITS[t]
                for h in range(IH):
                    for c0 in range(0, P * (t + 1), HALF):
                        c1 = min(c0 + HALF, P * (t + 1))
                        act.wait_ge(logit_up, n + 1)
                        if n >= 2:
                            act.wait_ge(logit_used, n - 1)
                        nc.scalar.activation(tmp[:, n % 2, 0:c1 - c0], psum[:, 2 + n % 2, 0:c1 - c0], ACT.Relu
                                             ).then_inc(logit_relu, 1)
                        n += 1

            for s in range(NSTEP + 2):
                if s == 16:
                    for k in range(KT):
                        prep_x(1, k)
                if s < 28:
                    split_z(s + 4)
                if s < NSTEP:
                    evacuate(s)
                for back in (2, 1):
                    b = s - back
                    if 0 <= b < NSTEP and b // 4 % 4 == KV:
                        t = b // 16 * 4 + b % 4
                        if back == 1:
                            keys_out(t)
                        elif t >= 2:
                            relus(t, min(s + 1, NSTEP))

            def split_main(m, slot, landings):
                if not isinstance(m, int) or m >= 4:
                    act.wait_ge(unit_up, m - 3)
                if isinstance(m, int) and m < 4:
                    act.wait_ge(z_up, NSTEP)
                split_hi(32 + m, slot % 2, landings, w_buf[:, 0, :, slot * P:(slot + 1) * P])

            for m in range(AHEAD):
                split_main(m, m, 16 + m // 2 + 1)

            def attention(half):
                def bank_out(key, dst, rows=slice(0, P), cols=HALF):
                    n = TR[key]
                    act.wait_ge(tr_up, n + 1)
                    return nc.scalar.copy(dst, psum[rows, 4 + n % 3, 0:cols])

                def cat(t):
                    j = t % 4
                    for g in range(2):
                        n = TR["cat", t, g]
                        act.wait_ge(tr_up, n + 1)
                        nc.scalar.copy(hid_buf[:, 0, 4 * g:4 * g + 4, j * P:(j + 1) * P],
                                       psum[:, 4 + n % 3, :].rearrange("p (k n) -> p k n", k=4)).then_inc(cat_hi, 1)
                        act.wait_ge(cat_hi, 2 * t + g + 1)
                        act.sem_inc(tr_read, 1)

                if half == 0:
                    act.wait_ge(z_up, NSTEP)
                def queries(t):
                    for g in range(2):
                        bank_out(("q", t, g), q_t[t % 2][:, 4 * g:4 * g + 4, :].rearrange("p h n -> p (h n)")
                                 ).then_inc(tr_read, 1)

                first, end = 32 * half, 32 * half + 32
                queries(4 * half)
                for a in range(first, end + 2):
                    t, h = a // 8, a % 8
                    if a < end:
                        if h == CAT_AT and t % 4:
                            cat(t - 1)
                        if h == Q_AT and t % 4 < 3:
                            queries(t + 1)
                        n = P * (t + 1)
                        if h == 0 and t % 4 >= 2:
                            act.wait_ge(att_norm, t - 1)
                        act.wait_ge(neg_up, a + 1)
                        if a >= first + 2:
                            act.wait_ge(tr_up, TR["p", a - 2, ((a - 2) // 8 + 4) // 4 - 1] + 1)
                        nc.scalar.activation(p_buf[:, a % 2, 0:n], s_buf[:, a % 2, 0:n], ACT.Exp,
                                             bias=neg_max[:, a % 2:a % 2 + 1], scale=HD ** -0.5,
                                             accum_out=row_sum[t % 2][:, h:h + 1]).then_inc(exp_up, 1)
                    if a >= first + 2:
                        b = a - 2
                        n = P * (b // 8 + 1)
                        if b >= 2:
                            act.wait_ge(pv_up, b - 1)
                        for g in range((b // 8 + 4) // 4):
                            cols = min(HALF, n - g * HALF)
                            bank_out(("p", b, g), pt_buf[:, b % 2, g * HALF:g * HALF + cols], cols=cols
                                     ).then_inc(tr_read, 1)
                cat(4 * half + 3)

            def units(first, count, job=None, last=False):
                def group(i):
                    for r in range(4):
                        if not (last and isinstance(i, int) and i == count // 4 - 1 and r >= 4 - AHEAD):
                            split_main(first + 4 * i + r + AHEAD, (r + AHEAD) % 4,
                                       16 + first // 2 + 2 * i + (r + AHEAD) // 2 + 1)
                        if job:
                            job(i, r)
                if first == 0:
                    for i in range(count // 4):
                        group(i)
                    return
                with act.Fori(0, count // 4 - last) as i:
                    group(i)
                if last:
                    group(count // 4 - 1)

            def final(first, half, name, g, dst):
                n0 = KT * PREP[name]

                def job(i, r):
                    k = 4 * i + r
                    wait_apart(act, unit_read, first + 4 * i + r + 1, passed_s)
                    prep(n0, k, flat(xt[half], None, k), dst, g)
                    square(n0, k, r % 2, flat(xt[half], None, k))
                return job

            def again(half, name, g, dst):
                n0 = KT * PREP[name]

                def job(i, r):
                    k = 4 * i + r
                    prep(n0, k, flat(xt[half], None, k), dst, g)
                    square(n0, k, r % 2, flat(xt[half], None, k))
                return job

            def swish(half, dst):
                def job(i, r):
                    k = 4 * i + r
                    n = 8 * half + k
                    act.wait_ge(act_in, n + 1)
                    act.wait_ge(act_lo, CREDIT + n - 1)
                    nc.scalar.activation(v_ring[:, r % 2], u_ring[:, r % 2], ACT.Silu).then_inc(act_silu, 1)
                    wait_apart(act, act_silu, CREDIT + n + 1, passed_s)
                    nc.scalar.activation(flat(dst, 0, k), v_ring[:, r % 2], ACT.Copy).then_inc(act_hi, 1)
                return job

            def both(*jobs):
                def job(i, r):
                    for j in jobs:
                        if j:
                            j(i, r)
                return job

            def conv_squares(half):
                def job(i, r):
                    k = 4 * i + r
                    act.wait_ge(conv_step, CONV * KT * (1 + half))
                    act.wait_ge(conv_sum, CREDIT + 8 * half + k - 1)
                    nc.scalar.activation(v_ring[:, r % 2], flat(c_buf, None, k), ACT.Square).then_inc(conv_sq, 1)
                return job

            def mlp(stage, half, hidden, following):
                first, ups = FIRST[stage, half], UPS[stage, half]
                for q in range(4):
                    def hidden_hi(i, r):
                        k = 4 * i + r
                        n = ups + 8 * q + k
                        act.wait_ge(unit_read, first + 16 * q + k + 1)
                        act.wait_ge(hid_lo, CREDIT + n - 1)
                        nc.scalar.activation(s_ring[:, r % 2], t_ring[:, r % 2], ACT.Square).then_inc(squared, 1)
                        wait_apart(act, squared, CREDIT + n + 1, passed_s)
                        nc.scalar.activation(flat(hidden, 0, k), s_ring[:, r % 2], ACT.Copy).then_inc(hid_hi, 1)

                    squares = None
                    if q == 3 and (stage, half) == ("ff1", 0):
                        act.wait_ge(act_lo, CREDIT + 8)
                        squares = conv_squares(1)
                    units(first + 16 * q, 8, both(hidden_hi, squares))
                    job = None
                    if q == 3:
                        down = first + 16 * q + 8
                        job = both(final(down, half, *following) if following else None,
                                   swish(1, hid_buf) if (stage, half) == ("ff1", 0) else None)
                    units(first + 16 * q + 8, 8, job, last=(q == 3 and (stage, half) == ("ff1", 1)))

            for name, half, _, count in STAGES:
                first = FIRST[name, half]
                if (name, half) == ("wout", 0):
                    attention(0)
                if (name, half) == ("wout", 1):
                    attention(1)
                if name == "wout" and half == 0:
                    units(first, 8, final(first, half, "ff0_0", G_FF0, h_buf))
                elif name == "wout":
                    act.wait_ge(unit_read, first)
                    units(first, 8, again(0, "pw1_0", G_OD, h_buf))
                elif name == "pw2":
                    units(first, 8, final(first, half, f"ff1_{half}", G_FF1, OPERAND[name, half][1]))
                elif name == "pw1":
                    def gate(part):
                        def job(i, r):
                            if r % 2:
                                act.wait_ge(unit_read, first + 8 * part + 4 * i + r + 1)
                                nc.scalar.activation(s_ring[:, r // 2], s_ring[:, r // 2], ACT.Sigmoid
                                                     ).then_inc(gate_up, 1)
                        return job
                    if half:
                        act.wait_ge(hid_lo, CREDIT + 64)
                        units(first, 8, both(gate(0), conv_squares(0)))
                        act.wait_ge(conv_sum, CREDIT + 8)
                        units(first + 8, 8, both(gate(1), swish(0, h_buf)))
                    else:
                        act.wait_ge(unit_read, first)
                        units(first, 8, gate(0))
                        units(first + 8, 8, both(gate(1), again(1, "ff0_1", G_FF0, hid_buf)))
                else:
                    if (name, half) == ("ff0", 1):
                        act.wait_ge(y_up, CREDIT + 9)
                    if (name, half) == ("ff1", 0):
                        act.wait_ge(y_up, CREDIT + 18)
                    mlp(name, half, OPERAND[name, half][1],
                        {("ff0", 1): ("pw1_1", G_OD, hid_buf)}.get((name, half)))

        @block.vector
        def _(dve):
            V = nc.vector
            chain = [0]

            def link(ins):
                chain[0] += 1
                ins.then_inc(dve_chain, 1)
                dve.wait_ge(dve_chain, chain[0])

            def rsqrt(dst, v, n):
                y, a = st_y[:, 0:n], st_a[:, 0:n]
                link(V.tensor_scalar(y.bitcast(I32), v.bitcast(I32), 1, None, ALU.logical_shift_right))
                link(V.tensor_scalar(y.bitcast(I32), y.bitcast(I32), -1.0, float(0x5F3759DF), ALU.mult, ALU.add))
                for step in range(3):
                    link(V.tensor_tensor(a, y, y, ALU.mult))
                    link(V.scalar_tensor_tensor(out=a, in0=a, scalar=-0.5, in1=v, op0=ALU.mult, op1=ALU.mult))
                    link(V.scalar_tensor_tensor(out=dst if step == 2 else y, in0=a, scalar=1.5, in1=y,
                                                op0=ALU.add, op1=ALU.mult))

            def rms_of(name, dst):
                dve.wait_ge(stat_up, STAT[name] + 1)
                link(V.tensor_scalar(st_v[:, 0:HT], psum[:, 7, 0:HT], 1.0 / D, EPS, ALU.mult, ALU.add))
                rsqrt(dst, st_v[:, 0:HT], HT)

            def rms_diag(name):
                rms_of(name, r_inv[:, 0:HT])
                for j in range(HT):
                    ins = V.tensor_scalar(diag[:, j * P:(j + 1) * P], ident[:], r_inv[:, j:j + 1], None, ALU.mult)
                    if j < HT - 1:
                        link(ins)
                ins.then_inc(stat_diag, 1)

            def rms_spread(name, dst):
                dve.wait_ge(stat_bc, BC[name] + 1)
                link(V.tensor_copy(dst[:], psum[:, 7, :]))

            def clear_sum():
                link(V.memset(sq_sum[:], 0.0))

            def prep(n0, k, ring, src, dst, g):
                n = n0 + k
                dve.wait_ge(prep_hi, n + 1)
                V.scalar_tensor_tensor(out=flat(dst, 1, k), in0=src, scalar=gflat(g, k),
                                       in1=flat(dst, 0, k).bitcast(F32), op0=ALU.mult, op1=ALU.subtract
                                       ).then_inc(prep_lo, 1)
                dve.wait_ge(prep_sq, n + 1)
                if not isinstance(n, int) or n >= 1:
                    dve.wait_ge(prep_sum, n)
                V.tensor_tensor(sq_sum[:], sq_sum[:], sq_ring[:, ring], ALU.add).then_inc(prep_sum, 1)

            def prep_x(half):
                clear_sum()
                for k in range(KT):
                    prep(KT * half, k, k % 2, x_in[:, k if half == 0 else 4 + k % 4], h_buf, G_EV)

            def rms_x(half):
                rms_of(f"z{half}", r_tok[:, 4 * half:4 * half + 4])
                dve.sem_inc(stat_diag, 1)

            dve.wait_ge(gains_in, 16)
            prep_x(0)

            dve.sem_inc(conv_sum, CREDIT)
            dve.wait_ge(consts_in, CONSTS_IN)
            dve.wait_ge(consts_up, CONSTS)
            link(V.tensor_copy(pos_f, pos_i[:]))
            ang, turns = qz[:, 0:256].rearrange("p (t f) -> p t f", t=8), qz[:, 256:512].rearrange("p (t f) -> p t f", t=8)
            for t in range(8):
                link(V.tensor_scalar(ang[:, t], inv_f[:], pos_f[:, t:t + 1], None, ALU.mult))
            TWO_PI = 2 * np.pi
            C1 = 6.28125
            C2 = float(np.float32(np.round((TWO_PI - C1) * 2 ** 19) / 2 ** 19))
            C3 = float(np.float32(TWO_PI - C1 - C2))
            MAGIC = 1.5 * 2 ** 23
            for dst, shift in ((sin, 0.0), (cos, 0.25)):
                link(V.tensor_scalar(turns, ang, float(1 / TWO_PI), shift, ALU.mult, ALU.add))
                link(V.tensor_scalar(turns, turns, MAGIC, None, ALU.add))
                link(V.tensor_scalar(turns, turns, MAGIC, None, ALU.subtract))
                link(V.scalar_tensor_tensor(out=dst[:], in0=turns, scalar=-C1, in1=ang, op0=ALU.mult, op1=ALU.add))
                link(V.scalar_tensor_tensor(out=dst[:], in0=turns, scalar=-C2, in1=dst[:], op0=ALU.mult, op1=ALU.add))
                link(V.scalar_tensor_tensor(out=dst[:], in0=turns, scalar=-C3, in1=dst[:], op0=ALU.mult, op1=ALU.add))
                if shift:
                    link(V.tensor_scalar(dst[:], dst[:], float(np.pi / 2), None, ALU.add))
                V.tensor_scalar(dst[:], dst[:], 3.1415925, -3.1415925, ALU.min, ALU.max).then_inc(rope_arg, 1)

            def rope_pair(k, kn, ki, kin, t):
                parts = [(k, kn, tmp[:, 1, 0:HD], HD // 2, cos[:, t, :], sin[:, t, :]),
                         (ki, kin, tmp[:, 1, HD:HD + ID], ID // 2, cos[:, t, ::2], sin[:, t, ::2])]
                for dst, src, other, h, c, s in parts:
                    V.tensor_tensor(dst[:, 0:h], src[:, 0:h], c, ALU.mult)
                    V.tensor_tensor(dst[:, h:2 * h], src[:, h:2 * h], c, ALU.mult)
                    V.tensor_tensor(other[:, 0:h], src[:, h:2 * h], s, ALU.mult)
                    ins = V.tensor_tensor(other[:, h:2 * h], src[:, 0:h], s, ALU.mult)
                link(ins)
                for dst, src, other, h, c, s in parts:
                    V.tensor_tensor(dst[:, 0:h], dst[:, 0:h], other[:, 0:h], ALU.subtract)
                    ins = V.tensor_tensor(dst[:, h:2 * h], dst[:, h:2 * h], other[:, h:2 * h], ALU.add)
                link(ins)

            def process_keys(s, t):
                dve.wait_ge(z_read, s + 1)
                if t >= 1:
                    dve.wait_ge(tr_up, TR["k", t - 1, 0] + 1)
                z = zt[:, t % 2]
                V.tensor_scalar(w_idx[t % 3], z[:, WI0:WI0 + IH], IDX_SCALE, None, ALU.mult)
                V.tensor_scalar(st_v[:, 0:1], st_k[:, t % 2, 0:1], 1.0 / HD, EPS, ALU.mult, ALU.add)
                link(V.tensor_scalar(st_v[:, 1:2], st_k[:, t % 2, 1:2], 1.0 / ID, EPS, ALU.mult, ALU.add))
                rsqrt(r_inv[:, 0:2], st_v[:, 0:2], 2)
                kn, kin = z[:, K0:K0 + HD], z[:, KI0:KI0 + ID]
                V.scalar_tensor_tensor(out=kn, in0=kn, scalar=r_inv[:, 0:1], in1=gh[:, 1, :],
                                       op0=ALU.mult, op1=ALU.mult)
                link(V.scalar_tensor_tensor(out=kin, in0=kin, scalar=r_inv[:, 1:2], in1=gh[:, 2, 0:ID],
                                            op0=ALU.mult, op1=ALU.mult))
                kr, kir = tmp[:, 0, 0:HD], tmp[:, 0, HD:HD + ID]
                rope_pair(kr, kn, kir, kin, t)
                V.tensor_copy(k_stack[:, 0:2, :], kr[:, None, :].broadcast_to([P, 2, HD]))
                link(V.tensor_copy(ki_stack[:, 0:2, :], kir[:, None, :].broadcast_to([P, 2, ID])))
                V.tensor_tensor(k_stack[:, 2, :], kr, k_stack[:, 0, :].bitcast(F32), ALU.subtract)
                V.tensor_tensor(ki_stack[:, 2, :], kir, ki_stack[:, 0, :].bitcast(F32), ALU.subtract
                                ).then_inc(z_proc, 1)

            def process_queries(s, t):
                dve.wait_ge(z_sq, t + 1)
                link(V.tensor_reduce(st_v[:, 0:HEADS], qz[:].rearrange("p (n d) -> p n d", n=HEADS), AX_X, ALU.add))
                link(V.tensor_scalar(st_v[:, 0:HEADS], st_v[:, 0:HEADS], 1.0 / HD, EPS, ALU.mult, ALU.add))
                rsqrt(r_q[:, t, :], st_v[:, 0:HEADS], HEADS)
                dve.sem_inc(z_proc, 1)

            def process_v(s, t):
                dve.wait_ge(z_vsq, t + 1)
                link(V.tensor_scalar(st_v[:, 0:1], vsum, 1.0 / HALF, EPS, ALU.mult, ALU.add))
                rsqrt(r_inv[:, 0:1], st_v[:, 0:1], 1)
                V.scalar_tensor_tensor(out=qz[:], in0=qz[:], scalar=r_inv[:, 0:1], in1=gvb[:],
                                       op0=ALU.mult, op1=ALU.mult).then_inc(z_proc, 1)

            def gate_v(t):
                dve.wait_ge(spat_up, t + 1)
                groups = psum[:, 7, :].rearrange("p (g d) -> p g d", g=GROUPS)
                link(V.tensor_tensor(tmp[:, 0].rearrange("p (g d) -> p g d", g=GROUPS), groups,
                                     bs[:][:, :, None].broadcast_to([P, GROUPS, GD]), ALU.add))
                V.tensor_tensor(b_tok[:, t, :], b_tok[:, t, :], tmp[:, 0], ALU.mult).then_inc(spat_used, 1)

            def index_scores(t):
                n = LOGITS[t]
                for h in range(IH):
                    for c0 in range(0, P * (t + 1), HALF):
                        c1 = min(c0 + HALF, P * (t + 1))
                        dve.wait_ge(logit_relu, n + 1)
                        dst, src, w = score[t][:, c0:c1], tmp[:, n % 2, 0:c1 - c0], w_idx[t % 3][:, h:h + 1]
                        if h == 0:
                            ins = V.tensor_scalar(dst, src, w, None, ALU.mult)
                        else:
                            back = 1 if c1 == P * (t + 1) and c0 == 0 else 2
                            dve.wait_ge(logit_used, n + 1 - back)
                            ins = V.scalar_tensor_tensor(out=dst, in0=src, scalar=w, in1=dst,
                                                         op0=ALU.mult, op1=ALU.add)
                        ins.then_inc(logit_used, 1)
                        n += 1
                dve.wait_ge(logit_used, n)
                last = score[t][:, P * t:P * (t + 1)]
                link(V.tensor_tensor(last, last, tri[:], ALU.add))

            def topk(tiles, at):
                for z, t in enumerate(tiles):
                    if not isinstance(at, int) or at:
                        wait_apart(dve, topk_step, 4 * at - 1 + z, passed_v)
                    V.max(top8[z], score[t][:]).then_inc(topk_step, 1)
                for z, t in enumerate(tiles):
                    wait_apart(dve, topk_step, 4 * at + 1 + z, passed_v)
                    V.match_replace(out=score[t][:], in_to_replace=top8[z], in_values=score[t][:], imm_value=TAKEN
                                    ).then_inc(topk_step, 1)

            rms_x(0)
            for s in range(NSTEP + 2):
                if s == 16:
                    prep_x(1)
                    gate_v(3)
                    rms_x(1)
                c, t = s // 4 % 4, s // 16 * 4 + s % 4
                if s < NSTEP:
                    if s == 0:
                        dve.wait_ge(rope_up, 2)
                    if c == KV:
                        process_keys(s, t)
                    elif c == QC:
                        process_queries(s, t)
                    elif c == UC:
                        dve.wait_ge(z_read, s + 1)
                        dve.sem_inc(z_proc, 1)
                    else:
                        process_v(s, t)
                b = s - 2
                if 0 <= b and b // 4 % 4 == KV and b // 16 * 4 + b % 4 >= 2:
                    index_scores(b // 16 * 4 + b % 4)
                b = s - 1
                if 0 <= b < NSTEP and b // 4 % 4 == VC and b != 15:
                    gate_v(b // 16 * 4 + b % 4)
                if 8 <= s < 16:
                    for z in range(3 if s < 12 else 1):
                        topk((2, 3), (s - 8) * 3 + z if s < 12 else s)

            def attention(half):
                def cat(t):
                    j = t % 4
                    for g in range(2):
                        n = TR["cat", t, g]
                        dve.wait_ge(cat_hi, 2 * t + g + 1)
                        cols = slice(j * P, (j + 1) * P)
                        V.tensor_tensor(hid_buf[:, 1, 4 * g:4 * g + 4, cols],
                                        psum[:, 4 + n % 3, :].rearrange("p (k n) -> p k n", k=4),
                                        hid_buf[:, 0, 4 * g:4 * g + 4, cols].bitcast(F32), ALU.subtract
                                        ).then_inc(cat_lo, 1)

                def normalise(t):
                    dve.wait_ge(exp_up, 8 * t + 8)
                    link(V.reciprocal(r_inv, row_sum[t % 2]))
                    dve.wait_ge(pv_up, 8 * t + 8)
                    V.tensor_tensor(a_tok[:].rearrange("p (n d) -> p n d", n=HEADS),
                                    psum[:, 7, :].rearrange("p (n d) -> p n d", n=HEADS),
                                    r_inv[:, :, None].broadcast_to([P, HEADS, HD]), ALU.mult).then_inc(att_norm, 1)

                dve.wait_ge(z_up, NSTEP)

                def split_queries(t):
                    dve.wait_ge(q_done, t + 1)
                    if t % 4:
                        dve.wait_ge(tr_up, TR["q", t - 1, 1] + 1)
                    link(V.tensor_tensor(q_tok[:, t], q_tok[:, t],
                                         r_q[:, t, :][:, :, None].broadcast_to([P, HEADS, HD]), ALU.mult))
                    link(V.tensor_copy(q_stack[:, :, 0, :], q_tok[:, t]))
                    V.tensor_tensor(q_stack[:, :, 1, :], q_tok[:, t], q_stack[:, :, 0, :].bitcast(F32), ALU.subtract
                                    ).then_inc(q_split, 1)

                def mask(t):
                    if t >= 2:
                        dve.wait_ge(topk_step, 4 * ROUNDS * (1 + 2 * half))
                        link(V.tensor_scalar(score[t][:], score[t][:], 0.9 * TAKEN, NEG, ALU.is_gt, ALU.mult))

                first, end = 32 * half, 32 * half + 32
                split_queries(4 * half)
                mask(4 * half)
                for a in range(first, end):
                    t, h = a // 8, a % 8
                    n = P * (t + 1)
                    dve.wait_ge(qk_up, a + 1)
                    if a >= 2:
                        dve.wait_ge(exp_up, a - 1)
                    logits = psum[:, 2 * (a % 2):2 * (a % 2) + 2, :].rearrange("p b n -> p (b n)")
                    s, m = s_buf[:, a % 2], row_max[:, a % 2:a % 2 + 1]
                    if t >= 2:
                        V.tensor_tensor_reduce(out=s[:, 0:n], in0=logits[:, 0:n], in1=score[t][:], scale=1.0,
                                               scalar=NEG, op0=ALU.add, op1=ALU.max, accum_out=m
                                               ).then_inc(qk_masked, 1)
                    else:
                        if t == 1:
                            V.tensor_copy(s[:, 0:P], logits[:, 0:P])
                        link(V.tensor_tensor(s[:, n - P:n], logits[:, n - P:n], tri[:], ALU.add))
                        V.tensor_reduce(m, s[:, 0:n], AX_X, ALU.max).then_inc(qk_masked, 1)
                    dve.wait_ge(qk_masked, a + 1)
                    V.tensor_scalar(neg_max[:, a % 2:a % 2 + 1], m, -(HD ** -0.5), None, ALU.mult
                                    ).then_inc(neg_up, 1)
                    if h == 2 and t % 4:
                        if t % 4 >= 2:
                            dve.wait_ge(cat_hi, 2 * (t - 1))
                        normalise(t - 1)
                    if h == CAT_AT and t % 4:
                        cat(t - 1)
                    if h == Q_AT - 1 and t % 4 < 3:
                        split_queries(t + 1)
                    if a < 16:
                        topk((2, 3), 16 + a)
                    if h == 7 and t % 4 < 3:
                        mask(t + 1)
                t = 4 * half + 3
                dve.wait_ge(cat_hi, 2 * t)
                normalise(t)
                cat(t)

            def units(first, count, *jobs):
                def group(i):
                    for r in range(4):
                        for job in jobs:
                            if job:
                                job(i, r)
                with dve.Fori(0, count // 4) as i:
                    group(i)

            def add_residual(first, half):
                def job(i, r):
                    m = first + 4 * i + r
                    x = flat(xt[half], None, 4 * i + r)
                    dve.wait_ge(unit_up, m + 1)
                    if first >= 2 * KT:
                        dve.wait_ge(unit_read, m - KT)
                    V.tensor_tensor(x, x, psum[:, r, :], ALU.add).then_inc(unit_read, 1)
                return job

            def final(half, name, g, dst):
                n0 = KT * PREP[name]

                def job(i, r):
                    prep(n0, 4 * i + r, r % 2, flat(xt[half], None, 4 * i + r), dst, g)
                return job

            def first_taps(half, quad):
                for z in range(4):
                    ct = 4 * quad + z
                    V.tensor_scalar(c_buf[:, ct, :], yflat(ct, 0), wdw[:, ct, 0:1], gain[:, B_DW, ct:ct + 1],
                                    ALU.mult, ALU.add).then_inc(conv_step, 1)

            def convolve(half, part):
                quad = part // 3

                def job(i, r):
                    for n in range(5 * r, 5 * r + 5):
                        k, ct = 1 + 10 * (part % 3) + 5 * i + n // 4, 4 * quad + n % 4
                        done = CONV * (KT * half + 4 * quad) + 4 + 40 * (part % 3) + 20 * i + n
                        dve.wait_ge(conv_step, done - 3)
                        V.scalar_tensor_tensor(out=c_buf[:, ct, :], in0=yflat(ct, k),
                                               scalar=wdw[:, ct, bass.ds(k, 1)], in1=c_buf[:, ct, :],
                                               op0=ALU.mult, op1=ALU.add).then_inc(conv_step, 1)
                return job

            def conv_squares(half):
                def job(i, r):
                    n = 8 * half + 4 * i + r
                    dve.wait_ge(conv_sq, n + 1)
                    dve.wait_ge(conv_sum, CREDIT + n)
                    V.tensor_tensor(c_sum[:], c_sum[:], v_ring[:, r % 2], ALU.add).then_inc(conv_sum, 1)
                return job

            def swish_arg(half):
                def job(i, r):
                    k = 4 * i + r
                    n = 8 * half + k
                    dve.wait_ge(act_silu, CREDIT + n - 1)
                    V.scalar_tensor_tensor(out=u_ring[:, r % 2], in0=flat(c_buf, None, k), scalar=gflat(G_CONV, k),
                                           in1=conv_bc[:], op0=ALU.mult, op1=ALU.mult).then_inc(act_in, 1)
                return job

            def mlp(stage, half, following):
                first, ups = FIRST[stage, half], UPS[stage, half]
                name = name_of(stage, half)
                conv = CONV_IN.get((stage, half))
                conv_half = int(half == 0)
                rms_diag(name)
                rms_spread(name, rms_bc)
                if (stage, half) == ("ff0", 1):
                    dve.wait_ge(y_up, CREDIT + 9)
                if conv:
                    dve.wait_ge(y_up, CREDIT + 9 * (conv_half + 1))
                for q in range(4):
                    up, down = first + 16 * q, first + 16 * q + 8

                    def relu_scaled(i, r):
                        k = 4 * i + r
                        n = ups + 8 * q + k
                        dve.wait_ge(unit_up, up + k + 1)
                        dve.wait_ge(squared, CREDIT + n - 1)
                        V.scalar_tensor_tensor(out=t_ring[:, r % 2], in0=psum[:, r, :], scalar=0.0, in1=rms_bc[:],
                                               op0=ALU.max, op1=ALU.mult).then_inc(unit_read, 1)

                    def more_topk(part):
                        def job(i, r):
                            topk((4, 7) if q < 2 else (5, 6), ROUNDS + 16 * q + 8 * part + 4 * i + r)
                        return job if (stage, half) == ("ff0", 0) else None

                    late = (stage, half) == ("ff1", 0)
                    if conv and q < 3:
                        if q == 0:
                            first_taps(conv_half, 0)
                        units(up, 8, relu_scaled, convolve(conv_half, 2 * q))
                        if q == 1:
                            first_taps(conv_half, 1)
                        units(down, 8, add_residual(down, half), convolve(conv_half, 2 * q + 1))
                        continue
                    if late:
                        link(V.memset(c_sum[:], 0.0))
                    units(up, 8, relu_scaled, more_topk(0), conv_squares(1) if late else None)
                    if q == 3:
                        if late:
                            rms_diag(conv)
                            rms_spread(conv, conv_bc)
                        if following:
                            clear_sum()
                        units(down, 8, add_residual(down, half), final(half, *following) if following else None,
                              swish_arg(1) if (stage, half) == ("ff1", 0) else None, more_topk(1))
                    else:
                        units(down, 8, add_residual(down, half), more_topk(1))

            for name, half, _, count in STAGES:
                first = FIRST[name, half]
                if (name, half) == ("wout", 0):
                    attention(0)
                    dve.wait_ge(x_full, 16)
                if (name, half) == ("wout", 1):
                    attention(1)
                if name == "wout" and half == 0:
                    clear_sum()
                    units(first, 8, add_residual(first, half), final(half, "ff0_0", G_FF0, h_buf))
                elif name == "wout":
                    dve.wait_ge(x_full, 32)
                    clear_sum()
                    units(first, 8, add_residual(first, half), final(0, "pw1_0", G_OD, h_buf))
                elif name == "pw2":
                    clear_sum()
                    units(first, 8, add_residual(first, half),
                          final(half, f"ff1_{half}", G_FF1, OPERAND[name, half][1]))
                elif name == "pw1":
                    rms_diag(f"pw1_{half}")
                    rms_spread(f"pw1_{half}", rms_bc)

                    def scale_pair(part):
                        def job(i, r):
                            p = 8 * half + 4 * part + 2 * i + r // 2
                            dve.wait_ge(unit_up, first + 8 * part + 4 * i + r + 1)
                            dve.wait_ge(y_up, CREDIT + p + half)
                            V.tensor_tensor((t_ring, s_ring)[r % 2][:, r // 2], psum[:, r, :], rms_bc[:], ALU.mult
                                            ).then_inc(unit_read, 1)
                        return job

                    if half:
                        dve.wait_ge(hid_lo, CREDIT + 64)
                        link(V.memset(c_sum[:], 0.0))
                        units(first, 8, scale_pair(0), conv_squares(0))
                        rms_diag("conv0")
                        rms_spread("conv0", conv_bc)
                        units(first + 8, 8, scale_pair(1), swish_arg(0))
                    else:
                        units(first, 8, scale_pair(0))
                        clear_sum()
                        units(first + 8, 8, scale_pair(1), final(1, "ff0_1", G_FF0, hid_buf))
                else:
                    mlp(name, half, {("ff0", 1): ("pw1_1", G_OD, hid_buf)}.get((name, half)))


def kernel(**inputs):
    import concourse.bacc as bacc
    from concourse.bass_utils import run_bass_kernel_spmd

    x = np.asarray(inputs["x"])
    w_in = np.asarray(inputs["ev_w_in"])[0]

    def units_of(w):
        rows, cols = w.shape
        return w.reshape(rows // D, KT, P, cols // P, P).transpose(0, 3, 2, 1, 4)

    q, kvi, u, v = (w_in[:, 0:512], w_in[:, 512:936], w_in[:, 936:1448], w_in[:, 1448:1960])
    kvi = np.concatenate([kvi, np.zeros((D, 512 - C0), w_in.dtype)], axis=1)
    z_blocks = [units_of(np.ascontiguousarray(a))[0] for a in (kvi, q, u, v)]

    def mlp_blocks(layer):
        up = units_of(np.asarray(inputs["ff_w1"])[layer])[0].reshape(4, 8, P, KT, P)
        down = units_of(np.asarray(inputs["ff_w2"])[layer])
        return np.stack([up, down], axis=1).reshape(64, P, KT, P)

    pw1 = units_of(np.asarray(inputs["od_w_pw1"])[0])[0].reshape(2, 8, P, KT, P).transpose(1, 0, 2, 3, 4)
    weights = np.concatenate(z_blocks + [units_of(np.asarray(inputs["ev_w_out"])[0])[0], mlp_blocks(0),
                                         pw1.reshape(16, P, KT, P), units_of(np.asarray(inputs["od_w_pw2"])[0])[0],
                                         mlp_blocks(1)])
    gains = np.stack([np.asarray(a).reshape(KT, P).T for a in (
        inputs["ev_g_norm"][0], inputs["ff_g_norm"][0], inputs["od_g_norm"][0], inputs["od_g_conv"][0],
        inputs["ff_g_norm"][1], inputs["od_b_dw"][0])], axis=1)
    g_kidx = np.concatenate([np.asarray(inputs["ev_g_kidx"])[0], np.zeros(HD - ID, np.float32)])
    g_head = np.stack([np.asarray(inputs["ev_g_q"])[0], np.asarray(inputs["ev_g_k"])[0], g_kidx])
    arrays = {
        "x_t": x[0].T.reshape(KT, P, SEQ),
        "positions": np.asarray(inputs["positions"])[0].reshape(8, P).T,
        "inv_freq": np.broadcast_to((10000.0 ** (-np.arange(HD // 2) * 2.0 / HD)).astype(np.float32), (P, HD // 2)),
        "weights": weights,
        "gains": gains,
        "g_head": np.broadcast_to(g_head[None], (P, 3, HD)),
        "g_vb": np.broadcast_to(np.asarray(inputs["ev_g_vb"])[0][None], (P, HALF)),
        "w_s": np.asarray(inputs["ev_w_s"])[0].transpose(2, 0, 1),
        "b_s": np.asarray(inputs["ev_b_s"])[0].T,
        "w_dw": np.asarray(inputs["od_w_dw"])[0].reshape(CONV, KT, P).transpose(2, 1, 0),
    }
    arrays = {name: np.ascontiguousarray(a) for name, a in arrays.items()}
    nc = bacc.Bacc("TRN2", target_bir_lowering=False, num_devices=1)
    args = [nc.dram_tensor(name, a.shape, mybir.dt.from_np(a.dtype), kind="ExternalInput").ap()
            for name, a in arrays.items()]
    out_t = nc.dram_tensor("out_t", (KT, P, SEQ), F32, kind="ExternalOutput").ap()
    build(nc, *args, out_t)
    r = run_bass_kernel_spmd(nc, [arrays], core_ids=[0])
    return np.ascontiguousarray(r.results[0]["out_t"].reshape(D, SEQ).T)[None]
```
